# Optimizing a Trainium2 kernel written in Bass

```python
import math
import jax, jax.numpy as jnp
from jax import lax
import numpy as np

D_MODEL = 1024
BATCH = 1
SEQ = 512
DEPTH = 2

N_EVEN = (DEPTH + 1) // 2
N_ODD = DEPTH // 2
RMS_EPS = 1e-6
ROPE_THETA = 10000.0
Q_BLOCK = 128
GRID_W = 64

D_FF = 2816

A_HEADS = 4
A_DH = 64
A_QK = A_HEADS * 2 * A_DH
A_V = A_HEADS * 2 * A_DH

B_HEADS = 8
B_DH = 64
B_W = B_HEADS * B_DH
NA_ROWS = 8
NA_COLS = 16

C_WIDTH = 512
C_BLOCKS = 8
C_BW = C_WIDTH // C_BLOCKS
CONV_W = 4
RG_C = 8.0

D_HEADS = 8
D_NOPE = 64
D_ROPE = 32
D_VDIM = 64
D_Q_RANK = 256
D_KV_RANK = 128

EVEN_IN = 2 * A_QK + A_V + 3 * B_W
EVEN_MIX = A_V + B_W
ODD_IN = 2 * C_WIDTH + D_Q_RANK + D_KV_RANK + D_ROPE
ODD_MIX = C_WIDTH + D_HEADS * D_VDIM

kernel_name = "hybrid_diff_na_rglru_mla_encoder"

def rmsnorm(x, g):
    xf = x.astype(jnp.float32)
    y = xf * lax.rsqrt(jnp.mean(xf * xf, axis=-1, keepdims=True) + RMS_EPS)
    return (y * g.astype(jnp.float32)).astype(x.dtype)

def swiglu(x, wg, wu, wd):
    return (jax.nn.silu(x @ wg) * (x @ wu)) @ wd

def split_cols(x, sizes):
    idx, acc = [], 0
    for s in sizes[:-1]:
        acc += s
        idx.append(acc)
    return jnp.split(x, idx, axis=-1)

def rope_tables(seq, dim):
    inv = 1.0 / (ROPE_THETA ** (jnp.arange(0, dim, 2, dtype=jnp.float32) / dim))
    ang = jnp.arange(seq, dtype=jnp.float32)[:, None] * inv[None, :]
    return jnp.cos(ang), jnp.sin(ang)

def apply_rope(x, cos, sin):
    half = cos.shape[1]
    shape = (1, cos.shape[0]) + (1,) * (x.ndim - 3) + (half,)
    c = cos.reshape(shape).astype(x.dtype)
    s = sin.reshape(shape).astype(x.dtype)
    x1, x2 = x[..., :half], x[..., half:]
    return jnp.concatenate([x1 * c - x2 * s, x1 * s + x2 * c], axis=-1)

def blocked_attention(q, k, v, scale):
    B_, S, H, Dk = q.shape
    Dv = v.shape[-1]
    nb = S // Q_BLOCK
    qb = q.reshape(B_, nb, Q_BLOCK, H, Dk).swapaxes(0, 1)

    def block(qi):
        s = jnp.einsum('bqhd,bkhd->bhqk', qi, k).astype(jnp.float32) * scale
        p = jax.nn.softmax(s, axis=-1)
        return jnp.einsum('bhqk,bkhe->bqhe', p.astype(v.dtype), v)

    o = lax.map(block, qb)
    return o.swapaxes(0, 1).reshape(B_, S, H * Dv)

def diff_attention(q, k, v, lam, subln_g, lam_init):
    B_, S, H = q.shape[:3]
    nb = S // Q_BLOCK
    scale = A_DH ** -0.5
    qb = q.reshape(B_, nb, Q_BLOCK, H, 2, A_DH).swapaxes(0, 1)

    def block(qi):
        s = jnp.einsum('bqhmd,bkhmd->bhmqk', qi, k).astype(jnp.float32) * scale
        p = jax.nn.softmax(s, axis=-1)
        w = p[:, :, 0] - lam * p[:, :, 1]
        return jnp.einsum('bhqk,bkhe->bqhe', w.astype(v.dtype), v)

    o = lax.map(block, qb).swapaxes(0, 1).reshape(B_, S, H, 2 * A_DH)
    o = rmsnorm(o, subln_g) * (1.0 - lam_init)
    return o.reshape(B_, S, H * 2 * A_DH)

def neighbourhood_attention(q, k, v, rpb):
    B_, S, H, dh = q.shape
    rows = S // GRID_W
    wr = min(NA_ROWS, rows)
    wc = NA_COLS
    r = jnp.arange(rows)
    r0 = jnp.clip(r - wr // 2, 0, rows - wr)
    key_rows = r0[:, None] + jnp.arange(wr)[None, :]
    c = jnp.arange(GRID_W)
    c0 = jnp.clip(c - wc // 2, 0, GRID_W - wc)
    col_in = (c[None, :] >= c0[:, None]) & (c[None, :] < c0[:, None] + wc)
    qg = q.reshape(B_, rows, GRID_W, H, dh)
    kg = k.reshape(B_, rows, GRID_W, H, dh)[:, key_rows]
    vg = v.reshape(B_, rows, GRID_W, H, dh)[:, key_rows]
    s = jnp.einsum('brqhd,brjkhd->bhrqjk', qg, kg).astype(jnp.float32) * (dh ** -0.5)
    dr = key_rows - r[:, None]
    dc = jnp.clip(c[None, :] - c[:, None], -(wc - 1), wc - 1)
    idx_r = (dr + NA_ROWS - 1)[:, None, :, None]
    idx_c = (dc + NA_COLS - 1)[None, :, None, :]
    bias = rpb.astype(jnp.float32)[:, idx_r, idx_c]
    s = jnp.where(col_in[:, None, :], s + bias[None], -jnp.inf)
    sh = s.shape
    p = jax.nn.softmax(s.reshape(sh[:4] + (wr * GRID_W,)), axis=-1).reshape(sh)
    o = jnp.einsum('bhrqjk,brjkhd->brqhd', p.astype(v.dtype), vg)
    return o.reshape(B_, S, H * dh)

def centred_conv(x, w, b):
    S = x.shape[1]
    lp = (CONV_W - 1) // 2
    rp = CONV_W - 1 - lp
    xp = jnp.pad(x, ((0, 0), (lp, rp), (0, 0)))
    return sum(xp[:, j:j + S] * w[j] for j in range(CONV_W)) + b

def rg_lru(x, w_a, b_a, w_x, b_x, lam, reverse):
    B_, S, C = x.shape
    xb = x.reshape(B_, S, C_BLOCKS, C_BW)
    r_t = jax.nn.sigmoid((jnp.einsum('bsnc,ncd->bsnd', xb, w_a).reshape(B_, S, C) + b_a).astype(jnp.float32))
    i_t = jax.nn.sigmoid((jnp.einsum('bsnc,ncd->bsnd', xb, w_x).reshape(B_, S, C) + b_x).astype(jnp.float32))
    log_a = -RG_C * r_t * jax.nn.softplus(-lam.astype(jnp.float32))
    a = jnp.exp(log_a)
    mult = jnp.sqrt(-jnp.expm1(2.0 * log_a))
    first = jnp.arange(S) == (S - 1 if reverse else 0)
    mult = jnp.where(first[None, :, None], 1.0, mult)
    bterm = mult * i_t * x.astype(jnp.float32)

    def comb(l, rr):
        a_l, b_l = l
        a_r, b_r = rr
        return a_l * a_r, a_r * b_l + b_r

    _, h = lax.associative_scan(comb, (a, bterm), reverse=reverse, axis=1)
    return h

def mla_attention(cq, ckv, kr, gq, gkv, wuq, wukv, cos, sin):
    B_, S, _ = cq.shape
    q = (rmsnorm(cq, gq) @ wuq).reshape(B_, S, D_HEADS, D_NOPE + D_ROPE)
    q = jnp.concatenate([q[..., :D_NOPE], apply_rope(q[..., D_NOPE:], cos, sin)], axis=-1)
    kv = (rmsnorm(ckv, gkv) @ wukv).reshape(B_, S, D_HEADS, D_NOPE + D_VDIM)
    k_pe = apply_rope(kr[:, :, None, :], cos, sin)
    k = jnp.concatenate([kv[..., :D_NOPE], jnp.broadcast_to(k_pe, (B_, S, D_HEADS, D_ROPE))], axis=-1)
    v = kv[..., D_NOPE:]
    return blocked_attention(q, k, v, (D_NOPE + D_ROPE) ** -0.5)

def even_mixer(h, w_in, w_out, lam_vec, subln_g, rpb, lam_init, cos, sin):
    B_, S, _ = h.shape
    qa, ka, va, qb, kb, vb = split_cols(h @ w_in, [A_QK, A_QK, A_V, B_W, B_W, B_W])
    qa = apply_rope(qa.reshape(B_, S, 2 * A_HEADS, A_DH), cos, sin).reshape(B_, S, A_HEADS, 2, A_DH)
    ka = apply_rope(ka.reshape(B_, S, 2 * A_HEADS, A_DH), cos, sin).reshape(B_, S, A_HEADS, 2, A_DH)
    lf = lam_vec.astype(jnp.float32)
    lam = jnp.exp(jnp.sum(lf[0] * lf[1])) - jnp.exp(jnp.sum(lf[2] * lf[3])) + lam_init
    oa = diff_attention(qa, ka, va.reshape(B_, S, A_HEADS, 2 * A_DH), lam, subln_g, lam_init)
    ob = neighbourhood_attention(qb.reshape(B_, S, B_HEADS, B_DH), kb.reshape(B_, S, B_HEADS, B_DH),
                                 vb.reshape(B_, S, B_HEADS, B_DH), rpb)
    return jnp.concatenate([oa, ob], axis=-1) @ w_out

def odd_mixer(h, w_in, w_out, conv_w, conv_b, rg_wa, rg_ba, rg_wx, rg_bx, rg_lam,
              gq, gkv, wuq, wukv, cos, sin):
    xc, gc, cq, ckv, kr = split_cols(h @ w_in, [C_WIDTH, C_WIDTH, D_Q_RANK, D_KV_RANK, D_ROPE])
    u = centred_conv(xc, conv_w, conv_b)
    hr = (rg_lru(u, rg_wa[0], rg_ba[0], rg_wx[0], rg_bx[0], rg_lam[0], False)
          + rg_lru(u, rg_wa[1], rg_ba[1], rg_wx[1], rg_bx[1], rg_lam[1], True))
    oc = jax.nn.gelu(gc) * hr.astype(h.dtype)
    od = mla_attention(cq, ckv, kr, gq, gkv, wuq, wukv, cos, sin)
    return jnp.concatenate([oc, od], axis=-1) @ w_out

def setup_inputs(seed: int = 0) -> dict:
    key = jax.random.key(seed)
    ks = iter(jax.random.split(key, 40))

    def nrm(shape, scale):
        return jax.random.normal(next(ks), shape, jnp.float32) * scale

    def gain(shape):
        return 1.0 + nrm(shape, 0.02)

    u = jax.random.uniform(next(ks), (N_ODD, 2, C_WIDTH), jnp.float32, 0.9, 0.999)
    a0 = u ** (1.0 / RG_C)
    return {
        "x": nrm((BATCH, SEQ, D_MODEL), 1.0),
        "ffn1_norm": gain((DEPTH, D_MODEL)),
        "ffn1_wg": nrm((DEPTH, D_MODEL, D_FF), D_MODEL ** -0.5),
        "ffn1_wu": nrm((DEPTH, D_MODEL, D_FF), D_MODEL ** -0.5),
        "ffn1_wd": nrm((DEPTH, D_FF, D_MODEL), D_FF ** -0.5),
        "mix_norm": gain((DEPTH, D_MODEL)),
        "ffn2_norm": gain((DEPTH, D_MODEL)),
        "ffn2_wg": nrm((DEPTH, D_MODEL, D_FF), D_MODEL ** -0.5),
        "ffn2_wu": nrm((DEPTH, D_MODEL, D_FF), D_MODEL ** -0.5),
        "ffn2_wd": nrm((DEPTH, D_FF, D_MODEL), D_FF ** -0.5),
        "final_norm": gain((D_MODEL,)),
        "ev_w_in": nrm((N_EVEN, D_MODEL, EVEN_IN), D_MODEL ** -0.5),
        "ev_w_out": nrm((N_EVEN, EVEN_MIX, D_MODEL), EVEN_MIX ** -0.5),
        "diff_lam": nrm((N_EVEN, 4, A_DH), 0.1),
        "diff_subln": gain((N_EVEN, 2 * A_DH)),
        "na_rpb": nrm((N_EVEN, B_HEADS, 2 * NA_ROWS - 1, 2 * NA_COLS - 1), 0.02),
        "od_w_in": nrm((N_ODD, D_MODEL, ODD_IN), D_MODEL ** -0.5),
        "od_w_out": nrm((N_ODD, ODD_MIX, D_MODEL), ODD_MIX ** -0.5),
        "conv_w": nrm((N_ODD, CONV_W, C_WIDTH), CONV_W ** -0.5),
        "conv_b": nrm((N_ODD, C_WIDTH), 0.01),
        "rg_wa": nrm((N_ODD, 2, C_BLOCKS, C_BW, C_BW), C_BW ** -0.5),
        "rg_ba": nrm((N_ODD, 2, C_WIDTH), 0.01),
        "rg_wx": nrm((N_ODD, 2, C_BLOCKS, C_BW, C_BW), C_BW ** -0.5),
        "rg_bx": nrm((N_ODD, 2, C_WIDTH), 0.01),
        "rg_lam": jnp.log(a0) - jnp.log1p(-a0),
        "mla_gq": gain((N_ODD, D_Q_RANK)),
        "mla_gkv": gain((N_ODD, D_KV_RANK)),
        "mla_wuq": nrm((N_ODD, D_Q_RANK, D_HEADS * (D_NOPE + D_ROPE)), D_Q_RANK ** -0.5),
        "mla_wukv": nrm((N_ODD, D_KV_RANK, D_HEADS * (D_NOPE + D_VDIM)), D_KV_RANK ** -0.5),
    }

def reference(x, ffn1_norm, ffn1_wg, ffn1_wu, ffn1_wd, mix_norm, ffn2_norm, ffn2_wg, ffn2_wu,
              ffn2_wd, final_norm, ev_w_in, ev_w_out, diff_lam, diff_subln, na_rpb, od_w_in,
              od_w_out, conv_w, conv_b, rg_wa, rg_ba, rg_wx, rg_bx, rg_lam, mla_gq, mla_gkv,
              mla_wuq, mla_wukv):
    S = x.shape[1]
    cos_a, sin_a = rope_tables(S, A_DH)
    cos_d, sin_d = rope_tables(S, D_ROPE)
    for l in range(DEPTH):
        x = x + 0.5 * swiglu(rmsnorm(x, ffn1_norm[l]), ffn1_wg[l], ffn1_wu[l], ffn1_wd[l])
        h = rmsnorm(x, mix_norm[l])
        if l % 2 == 0:
            i = l // 2
            lam_init = 0.8 - 0.6 * math.exp(-0.3 * l)
            x = x + even_mixer(h, ev_w_in[i], ev_w_out[i], diff_lam[i], diff_subln[i], na_rpb[i],
                               lam_init, cos_a, sin_a)
        else:
            i = l // 2
            x = x + odd_mixer(h, od_w_in[i], od_w_out[i], conv_w[i], conv_b[i], rg_wa[i], rg_ba[i],
                              rg_wx[i], rg_bx[i], rg_lam[i], mla_gq[i], mla_gkv[i], mla_wuq[i],
                              mla_wukv[i], cos_d, sin_d)
        x = x + 0.5 * swiglu(rmsnorm(x, ffn2_norm[l]), ffn2_wg[l], ffn2_wu[l], ffn2_wd[l])
    return rmsnorm(x, final_norm)


_drawn_inputs = setup_inputs


def setup_inputs(seed=0):
    import zlib

    import numpy as np

    out = dict(_drawn_inputs(seed))
    spreads = {}
    factors = {'ffn1_norm': 3.751,
     'ffn2_norm': 5.882,
     'final_norm': 22.756,
     'diff_subln': 3.957,
     'na_rpb': 23.516,
     'rg_ba': 200.0,
     'rg_bx': 200.0,
     'mla_gq': 8.0,
     'mla_gkv': 8.0,
     'conv_b': 64.0,
     'rg_wa': 47.248,
     'rg_wx': 12.385,
     'rg_lam': 35.272}
    for name, (base, spread) in spreads.items():
        noise = np.random.default_rng([zlib.crc32(name.encode()), seed]).standard_normal(out[name].shape)
        drawn = base * np.exp(spread * noise) if base else spread * noise
        out[name] = __import__('jax').numpy.asarray(drawn.astype(out[name].dtype))
    for name, factor in factors.items():
        out[name] = (out[name] * factor).astype(out[name].dtype)
    return out
```

```python
from contextlib import ExitStack

import numpy as np

import concourse.bass as bass
from concourse import mybir

ACT = mybir.ActivationFunctionType
ALU = mybir.AluOpType
AX = mybir.AxisListType.X
F32 = mybir.dt.float32
F32R = mybir.dt.float32r

P = 128
SEQ, D, FF = 512, 1024, 2816
KD = D // P
TT = SEQ // P
NF = FF // P
PAIRS = NF // 2
UNIT = 2048
EPS = 1e-6
GRID_R, GRID_C = 8, 64
WIN = 32
WSTART = (0, 8, 24, 32)
MTYPE = (0, 1, 1, 2)
NEG = -1.0e30

FFN_UNITS = 3 * PAIRS
EVEN_UNITS = 12 + 4
ODD_UNITS = 6 + 3 + 4
U_FFN = (0, FFN_UNITS + EVEN_UNITS, 2 * FFN_UNITS + EVEN_UNITS, 3 * FFN_UNITS + EVEN_UNITS + ODD_UNITS)
U_EVEN = FFN_UNITS
U_ODD = U_FFN[2] + FFN_UNITS
N_UNITS = 4 * FFN_UNITS + EVEN_UNITS + ODD_UNITS


def build_trunk(nc, xT, units, gains, consts, colvec, lamvec, rpb, ident_d, perm_d, rope_a, rope_d, masks_d, out):
    ctx = ExitStack()
    with ctx:
        def sem(name):
            return ctx.enter_context(nc.semaphore(name))

        def sb(name, shape, dt=F32, stack=ctx):
            return stack.enter_context(nc.sbuf_tensor(name, shape, dt))

        x = sb("x", [P, KD, SEQ])
        xgh = sb("xgh", [P, KD, SEQ], F32R)
        xgl = sb("xgl", [P, KD, SEQ], F32R)
        raw = sb("raw", [P, 2, UNIT])
        wh = sb("wh", [P, 2, UNIT], F32R)
        wl = sb("wl", [P, 2, UNIT], F32R)
        rB = sb("rB", [P, SEQ])
        sqt = sb("sqt", [P, 2, SEQ])
        std = sqt[:, 0, :]
        acc = sb("acc", [P, SEQ])
        ones = sb("ones", [P, P])
        ident = sb("ident", [P, P])
        gain = sb("gain", [P, 7 * KD])
        cvec = sb("cvec", [P, 48])
        small = sb("small", [P, 88])

        ffn_mem = ExitStack()
        ah = sb("ah", [P, NF, SEQ], F32R, ffn_mem)
        al = sb("al", [P, NF, SEQ], F32R, ffn_mem)
        tg = sb("tg", [P, 2, SEQ], F32, ffn_mem)
        sg = sb("sg", [P, 2, SEQ], F32, ffn_mem)
        ffn_mem.close()

        even_mem = ExitStack()
        oA = sb("oA", [P, TT, 512], F32, even_mem)
        relb = sb("relb", [P, 8, 8, 48], F32, even_mem)
        mask = acc[:, 0:3 * WIN].rearrange("p (m c) -> p m c", m=3)
        diff_mem = ExitStack()
        cosA = sb("cosA", [P, SEQ], F32, diff_mem)
        sinA = sb("sinA", [P, SEQ], F32, diff_mem)
        permA = sb("permA", [P, P], F32, diff_mem)
        qah = sb("qah", [P, 4, SEQ], F32R, diff_mem)
        qal = sb("qal", [P, 4, SEQ], F32R, diff_mem)
        kah = sb("kah", [P, 4, SEQ], F32R, diff_mem)
        kal = sb("kal", [P, 4, SEQ], F32R, diff_mem)
        vah = sb("vah", [P, TT, 512], F32R, diff_mem)
        val = sb("val", [P, TT, 512], F32R, diff_mem)
        q32 = sb("q32", [P, 2, SEQ], F32, diff_mem)
        qc = sb("qc", [P, 2, SEQ], F32, diff_mem)
        qs = sb("qs", [P, 2, SEQ], F32, diff_mem)
        eA = sb("eA", [P, 2, 2, SEQ], F32, diff_mem)
        aTh = sb("aTh", [P, 2, SEQ], F32R, diff_mem)
        aTl = sb("aTl", [P, 2, SEQ], F32R, diff_mem)
        lamb = eA[:, 0, 0, 0:256]
        junk = sb("junk", [P, P], F32, diff_mem)
        lamp = junk[:, :].rearrange("p (a e) -> p a e", a=2)
        diff_mem.close()
        oB = sb("oB", [P, TT, 512], F32, even_mem)
        qbh = sb("qbh", [P, 4, SEQ], F32R, even_mem)
        qbl = sb("qbl", [P, 4, SEQ], F32R, even_mem)
        kbh = sb("kbh", [P, 4, SEQ], F32R, even_mem)
        kbl = sb("kbl", [P, 4, SEQ], F32R, even_mem)
        vbh = sb("vbh", [P, TT, 512], F32R, even_mem)
        vbl = sb("vbl", [P, TT, 512], F32R, even_mem)
        qb_mem = ExitStack()
        qb32 = sb("qb32", [P, 2, SEQ], F32, qb_mem)
        qb_mem.close()
        p3 = sb("p3", [P, 2, 2, 384], F32, even_mem)
        bm = sb("bm", [P, 8, 8, WIN], F32, even_mem)
        sB = sqt[:, :, :].rearrange("p s (h k) -> p s h k", h=2)
        bTh = sb("bTh", [P, 2, 2, 384], F32R, even_mem)
        bTl = sb("bTl", [P, 2, 2, 384], F32R, even_mem)
        even_mem.close()

        odd_mem = ExitStack()
        cq_mem = ExitStack()
        cq = sb("cq", [P, 3, SEQ], F32, cq_mem)
        cqh = sb("cqh", [P, 3, SEQ], F32R, cq_mem)
        cql = sb("cql", [P, 3, SEQ], F32R, cq_mem)
        kpe = sb("kpe", [96, SEQ], F32, cq_mem)
        cq_mem.close()
        eD = sb("eD", [P, 2, 2, SEQ], F32, odd_mem)
        oD = sb("oD", [P, TT, 512], F32, odd_mem)
        rest = sb("rest", [P, 1024], F32, odd_mem)
        th_mem = ExitStack()
        th = sb("th", [P, 8, SEQ], F32, th_mem)
        th_mem.close()
        u_mem = ExitStack()
        uh = sb("uh", [P, 4, SEQ], F32R, u_mem)
        ul = sb("ul", [P, 4, SEQ], F32R, u_mem)
        u_mem.close()
        dT_mem = ExitStack()
        dTh = sb("dTh", [P, 2, 2, 512], F32R, dT_mem)
        dTl = sb("dTl", [P, 2, 2, 512], F32R, dT_mem)
        dT_mem.close()
        cosD = sb("cosD", [96, SEQ], F32, odd_mem)
        sinD = sb("sinD", [96, SEQ], F32, odd_mem)
        permD = sb("permD", [96, 96], F32, odd_mem)
        qd32 = sb("qd32", [96, 2, SEQ], F32, odd_mem)
        qdc = sb("qdc", [96, 2, SEQ], F32, odd_mem)
        qds = sb("qds", [96, 2, SEQ], F32, odd_mem)
        rg_mem = ExitStack()
        xcp = sb("xcp", [P, 4, SEQ + 3], F32, rg_mem)
        gc = sb("gc", [P, 4, SEQ], F32, rg_mem)
        u32 = sb("u32", [P, 4, SEQ], F32, rg_mem)
        ra = sb("ra", [P, 8, SEQ], F32, rg_mem)
        iu = sb("iu", [P, 8, SEQ], F32, rg_mem)
        rg_mem.close()
        qdh = sb("qdh", [96, 8, SEQ], F32R, odd_mem)
        qdl = sb("qdl", [96, 8, SEQ], F32R, odd_mem)
        kdh = sb("kdh", [96, 8, SEQ], F32R, odd_mem)
        kdl = sb("kdl", [96, 8, SEQ], F32R, odd_mem)
        vdh, vdl = xgh[:, 4:8, :], xgl[:, 4:8, :]
        odd_mem.close()

        ps = ctx.enter_context(nc.psum_tensor("ps", [P, 8, 512], F32))

        C_EPS, C_NLAM = 0, 1
        C_RN = 4
        C_NMX, C_SUM, C_REC, C_CF = 12, 16, 20, 24
        C_SS, C_RS = 28, 44
        C_LAM = 60
        C_M8, C_P8 = 64, 72
        C_TMP = 12
        recs = small[:, 80:88]
        V_CW, V_CB, V_BA, V_BX, V_LAM, V_GQ, V_GKV, V_SUB = 0, 16, 20, 28, 36, 44, 46, 47

        def col(c, n=1):
            return small[:, c:c + n]

        def vec(c, n=1):
            return cvec[:, c:c + n]

        x_in = sem("x_in")
        const_in = sem("const_in")
        ones_set = sem("ones_set")
        raw_in = [sem("raw_in0"), sem("raw_in1")]
        w_hi = sem("w_hi")
        w_lo = sem("w_lo")
        w_half = sem("w_half")
        x_new = sem("x_new")
        xg_hi = sem("xg_hi")
        xg_lo = sem("xg_lo")
        sq_done = sem("sq_done")
        sq_sum = sem("sq_sum")
        ssum_done = sem("ssum_done")
        std_done = sem("std_done")
        rstd = sem("rstd")
        tg_done = sem("tg_done")
        silu_done = sem("silu_done")
        s2_done = sem("s2_done")
        a32_done = sem("a32_done")
        a_hi = sem("a_hi")
        a_lo = sem("a_lo")
        y_done = sem("y_done")
        out_done = sem("out_done")
        stored = sem("stored")
        setup = sem("setup")

        even_in = sem("even_in")
        odd_in = sem("odd_in")


        def split_hi(act, c, p=0):
            act.wait_ge(raw_in[c % 2], 16 * p + 16 * (c // 2 + 1))
            if c >= 2:
                act.wait_ge(w_half, 4 * p + 2 * (c - 1))
            nc.scalar.activation(wh[:, c % 2, :], raw[:, c % 2, :], ACT.Copy).then_inc(w_hi, 1)

        def split_lo(dve, c, p=0):
            dve.wait_ge(w_hi, 2 * p + c + 1)
            nc.vector.tensor_tensor(wl[:, c % 2, :], raw[:, c % 2, :], wh[:, c % 2, :].bitcast(F32),
                                    ALU.subtract).then_inc(w_lo, 1)

        def three(dst, lh, ll, rh, rl, first, last):
            nc.tensor.matmul(dst, lh, rh, start=first, stop=False)
            nc.tensor.matmul(dst, lh, rl, start=False, stop=False)
            return nc.tensor.matmul(dst, ll, rh, start=False, stop=last)

        def block_T(pe, dst, c, m, width=P, step=256, nt=KD, wait_x=None):
            s = c % 2
            for k in range(nt):
                if wait_x is not None:
                    pe.wait_ge(xg_lo, wait_x + k + 1)
                o = k * step + m * P
                mm = three(dst, wh[:, s, o:o + width], wl[:, s, o:o + width],
                           xgh[:, k, :], xgl[:, k, :], k == 0, k == nt - 1)
            return mm

        def finish_dve(dve, n, scale, last_unit):
            for b in range(KD):
                if b < KD - 1:
                    dve.wait_ge(y_done, 7 * (n - 1) + b + 1)
                else:
                    dve.wait_ge(w_half, 2 * (last_unit + 1))
                nc.vector.scalar_tensor_tensor(x[:, b, :], ps[:, b, :], scale, x[:, b, :],
                                               ALU.mult, ALU.add).then_inc(x_new, 1)
                if b >= 1 and n < 6:
                    lo_x(dve, n, b - 1)
            if n < 6:
                lo_x(dve, n, KD - 1)

        def lo_x(dve, n, b):
            dve.wait_ge(xg_hi, 8 * n + b + 1)
            nc.vector.scalar_tensor_tensor(xgl[:, b, :], x[:, b, :], gain[:, n * KD + b:n * KD + b + 1],
                                           xgh[:, b, :].bitcast(F32), ALU.mult, ALU.subtract).then_inc(xg_lo, 1)

        def finish_act(act, n, last_unit=None):
            for b in range(KD):
                if n:
                    act.wait_ge(x_new, 8 * (n - 1) + b + 1)
                if n < 6:
                    if b >= 6 and last_unit is not None:
                        act.wait_ge(w_half, 2 * (last_unit + 1))
                    nc.scalar.activation(xgh[:, b, :], x[:, b, :], ACT.Copy,
                                         scale=gain[:, n * KD + b:n * KD + b + 1]).then_inc(xg_hi, 1)
                if b == 0 and n:
                    act.wait_ge(ssum_done, n)
                if b == 1 and n:
                    act.wait_ge(sq_sum, 7 * n)
                if b >= 3:
                    act.wait_ge(sq_sum, 7 * n + b - 2)
                dst = acc[:, :] if b == 0 else sqt[:, b % 2, :]
                nc.scalar.activation(dst, x[:, b, :], ACT.Square).then_inc(sq_done, 1)

        def finish_pool(pool, n):
            for b in range(1, KD):
                pool.wait_ge(sq_done, 8 * n + b + 1)
                if b >= 2:
                    pool.wait_ge(sq_sum, 7 * n + b - 1)
                nc.gpsimd.tensor_tensor(acc[:, :], acc[:, :], sqt[:, b % 2, :], ALU.add).then_inc(sq_sum, 1)

        def norm_pe(pe, n, bank):
            pe.wait_ge(sq_sum, 7 * (n + 1))
            nc.tensor.matmul(ps[:, bank, :], ones[:, :], acc[:, :], start=True, stop=True).then_inc(ssum_done, 1)

        def norm_act(act, n, bank):
            act.wait_ge(ssum_done, n + 1)
            if n:
                act.wait_ge(rstd, n)
            nc.scalar.activation(std, ps[:, bank, :], ACT.Sqrt, bias=col(C_EPS),
                                 scale=1.0 / D).then_inc(std_done, 1)

        def norm_dve(dve, n):
            dve.wait_ge(std_done, n + 1)
            nc.vector.reciprocal(rB[:, :], std).then_inc(rstd, 1)


        def ffn_up_pe(pe, f, B, n, p):
            first = isinstance(p, int)
            c0, c1 = B, B + 1
            pe.wait_ge(w_lo, 2 * p + c0 + 1)
            if not first:
                pe.wait_ge(tg_done, 2 * p + 22 * f)
            for m in range(2):
                block_T(pe, ps[:, m, :], c0, m, wait_x=8 * n if first and m == 0 else None).then_inc(w_half, 1)
                if first and m == 0:
                    norm_pe(pe, n, 4)
            pe.wait_ge(w_lo, 2 * p + c1 + 1)
            if not first:
                pe.wait_ge(a32_done, 2 * p + 22 * f)
            for m in range(2):
                block_T(pe, ps[:, 2 + m, :], c1, m).then_inc(w_half, 1)

        def down_pe(pe, c, p, kt, src_h, src_l, first):
            s = c % 2
            pe.wait_ge(w_lo, 2 * p + c + 1)
            for k2 in range(2):
                for b in (4, 5, 6, 7, 0, 1, 2, 3):
                    o = k2 * D + b * P
                    mm = three(ps[:, b, :], wh[:, s, o:o + P], wl[:, s, o:o + P],
                               src_h[:, bass.ds(kt + k2, 1), :], src_l[:, bass.ds(kt + k2, 1), :],
                               first and k2 == 0, False)
                mm.then_inc(w_half, 1)

        def down_last_pe(pe, c, kt, src_h, src_l):
            s = c % 2
            pe.wait_ge(w_lo, c + 1)
            for b in range(KD):
                for k2 in range(2):
                    o = k2 * D + b * P
                    mm = three(ps[:, b, :], wh[:, s, o:o + P], wl[:, s, o:o + P],
                               src_h[:, kt + k2, :], src_l[:, kt + k2, :], False, k2 == 1)
                if b < KD - 1:
                    mm.then_inc(y_done, 1)
                else:
                    mm.then_inc(w_half, 2)

        def ffn_pe(pe, f, B, n):
            ffn_up_pe(pe, f, B, n, 0)
            with pe.Fori(1, PAIRS) as p:
                ffn_up_pe(pe, f, B, n, p)
            c = B + 2 * PAIRS
            pe.wait_ge(a_lo, 22 * f + NF - 2)
            pe.wait_ge(std_done, n + 1)
            s = c % 2
            pe.wait_ge(w_lo, c + 1)
            for k2 in range(2):
                for b in (4, 5, 6, 7, 0, 1, 2, 3):
                    if k2 == 0 and b == 0:
                        pe.wait_ge(a32_done, 22 * (f + 1))
                    o = k2 * D + b * P
                    mm = three(ps[:, b, :], wh[:, s, o:o + P], wl[:, s, o:o + P],
                               ah[:, k2, :], al[:, k2, :], k2 == 0, False)
                mm.then_inc(w_half, 1)
            pe.wait_ge(a_lo, 22 * (f + 1))
            with pe.Fori(0, (PAIRS - 3) // 2) as j:
                for t in range(2):
                    down_pe(pe, c + 1 + t, j, 4 * j + 2 + 2 * t, ah, al, False)
            down_pe(pe, c + 9, 0, 18, ah, al, False)
            down_last_pe(pe, c + 10, 20, ah, al)

        def ffn_act(act, f, B, n, last):
            def pair(p, at_start):
                split_hi(act, B + 1, p)
                if at_start:
                    norm_act(act, n, 4)
                for m in range(2):
                    act.wait_ge(tg_done, 2 * p + 22 * f + m + 1)
                    nc.scalar.activation(sg[:, m, :], tg[:, m, :], ACT.Silu).then_inc(silu_done, 1)
                split_hi(act, B + 2, p)
                for m in range(2):
                    act.wait_ge(a32_done, 2 * p + 22 * f + m + 1)
                    nc.scalar.activation(ah[:, bass.ds(2 * p + m, 1), :], tg[:, m, :], ACT.Copy).then_inc(a_hi, 1)

            pair(0, True)
            with act.Fori(1, PAIRS) as p:
                pair(p, False)
            c = B + 2 * PAIRS
            with act.Fori(0, (PAIRS - 1) // 2) as j:
                split_hi(act, c + 1, j)
                split_hi(act, c + 2, j)
            if not last:
                split_hi(act, c + PAIRS)
            finish_act(act, n + 1)

        def ffn_dve(dve, f, B, n, last):
            def pair(p, at_start):
                split_lo(dve, B + 1, p)
                if at_start:
                    norm_dve(dve, n)
                    dve.wait_ge(rstd, n + 1)
                if f or not at_start:
                    dve.wait_ge(a_lo, 2 * p + 22 * f)
                for m in range(2):
                    dve.wait_ge(w_half, 4 * p + 2 * B + m + 1)
                    nc.vector.tensor_tensor(tg[:, m, :], ps[:, m, :], rB[:, :], ALU.mult).then_inc(tg_done, 1)
                split_lo(dve, B + 2, p)
                for m in range(2):
                    dve.wait_ge(w_half, 4 * p + 2 * B + m + 3)
                    dve.wait_ge(s2_done, 2 * p + 22 * f + m + 1)
                    nc.vector.tensor_tensor(tg[:, m, :], ps[:, 2 + m, :], sg[:, m, :], ALU.mult).then_inc(a32_done, 1)
                for m in range(2):
                    dve.wait_ge(a_hi, 2 * p + 22 * f + m + 1)
                    nc.vector.tensor_tensor(al[:, bass.ds(2 * p + m, 1), :], tg[:, m, :],
                                            ah[:, bass.ds(2 * p + m, 1), :].bitcast(F32),
                                            ALU.subtract).then_inc(a_lo, 1)

            pair(0, True)
            with dve.Fori(1, PAIRS) as p:
                pair(p, False)
            c = B + 2 * PAIRS
            with dve.Fori(0, (PAIRS - 1) // 2) as j:
                split_lo(dve, c + 1, j)
                split_lo(dve, c + 2, j)
            if not last:
                split_lo(dve, c + PAIRS)
            finish_dve(dve, n + 1, 0.5, c + PAIRS - 1)

        def ffn_pool(pool, f, n):
            pool.wait_ge(rstd, n + 1)
            with pool.Fori(0, PAIRS) as p:
                for m in range(2):
                    pool.wait_ge(silu_done, 2 * p + 22 * f + m + 1)
                    nc.gpsimd.tensor_tensor(sg[:, m, :], sg[:, m, :], rB[:, :], ALU.mult).then_inc(s2_done, 1)
            finish_pool(pool, n + 1)

        a_done = sem("a_done")
        ah_done = sem("ah_done")
        al_done = sem("al_done")
        asq_done = sem("asq_done")
        asqo_done = sem("asqo_done")
        bm_done = sem("bm_done")
        bt_done = sem("bt_done")
        cq_hi = sem("cq_hi")
        cq_lo = sem("cq_lo")
        cqn_done = sem("cqn_done")
        crs_done = sem("crs_done")
        cs_done = sem("cs_done")
        csq_done = sem("csq_done")
        csq_sum = sem("csq_sum")
        cstd_done = sem("cstd_done")
        ea_done = sem("ea_done")
        gate_done = sem("gate_done")
        gelu_done = sem("gelu_done")
        h_done = sem("h_done")
        hs_done = sem("hs_done")
        in_read = sem("in_read")
        iu_done = sem("iu_done")
        kd_hi = sem("kd_hi")
        kd_lo = sem("kd_lo")
        kd_ps = sem("kd_ps")
        lam_done = sem("lam_done")
        lam_exp = sem("lam_exp")
        mask_in = sem("mask_in")
        mix_hi = sem("mix_hi")
        mix_lo = sem("mix_lo")
        mt_done = sem("mt_done")
        mult_done = sem("mult_done")
        mxa_done = sem("mxa_done")
        mxraw = sem("mxraw")
        oa_done = sem("oa_done")
        oan_done = sem("oan_done")
        oc_done = sem("oc_done")
        omix_hi = sem("omix_hi")
        omix_lo = sem("omix_lo")
        omt_done = sem("omt_done")
        one_done = sem("one_done")
        p3_zero = sem("p3_zero")
        pa_done = sem("pa_done")
        pad_done = sem("pad_done")
        q32_done = sem("q32_done")
        qa_hi = sem("qa_hi")
        qa_lo = sem("qa_lo")
        qb32_done = sem("qb32_done")
        qb_hi = sem("qb_hi")
        qb_lo = sem("qb_lo")
        qc_done = sem("qc_done")
        qd32_done = sem("qd32_done")
        qd_hi = sem("qd_hi")
        qd_lo = sem("qd_lo")
        qd_ps = sem("qd_ps")
        qdc_done = sem("qdc_done")
        qdr_done = sem("qdr_done")
        qds_done = sem("qds_done")
        qr_done = sem("qr_done")
        qs_done = sem("qs_done")
        rcol_done = sem("rcol_done")
        rcol_read = sem("rcol_read")
        reca_done = sem("reca_done")
        rot_done = sem("rot_done")
        rotd_done = sem("rotd_done")
        rsa_done = sem("rsa_done")
        sa_done = sem("sa_done")
        setup_act_done = sem("setup_act_done")
        sig_done = sem("sig_done")
        ssa_done = sem("ssa_done")
        ta_done = sem("ta_done")
        th_done = sem("th_done")
        tmax_done = sem("tmax_done")
        u_done = sem("u_done")
        u_hi = sem("u_hi")
        u_lo = sem("u_lo")
        va_hi = sem("va_hi")
        va_lo = sem("va_lo")
        vb_hi = sem("vb_hi")
        vb_lo = sem("vb_lo")
        vt_done = sem("vt_done")
        vd_hi = sem("vd_hi")
        vd_lo = sem("vd_lo")
        vd_ps = sem("vd_ps")
        vv_done = sem("vv_done")
        wa_done = sem("wa_done")
        PAIR_SEMS = ("scores", "scores_read", "max", "exp", "rec", "turned", "hi", "lo", "pv", "o")
        SN = {n: sem("n_" + n) for n in PAIR_SEMS}
        SM = {n: sem("m_" + n) for n in PAIR_SEMS}
        SM["scores_read"] = SM["exp"]

        TMP = [small[:, C_TMP + 8 * i:C_TMP + 8 * i + 8] for i in range(6)]
        NLAM, EXPL, SS1, SS2, POLY, SPT = TMP

        def setup_act(act):
            act.wait_ge(setup, 2)
            nc.scalar.activation(EXPL, EXPL, ACT.Exp, scale=-1.0).then_inc(setup_act_done, 1)

        def setup_dve(dve):
            n = [0]

            def step(ins):
                n[0] += 1
                ins.then_inc(setup, 1)
                dve.wait_ge(setup, n[0])

            lam = vec(V_LAM, 8)
            step(nc.vector.tensor_scalar(NLAM, lam, -1.0, None, ALU.mult))
            step(nc.vector.tensor_tensor(EXPL, NLAM, lam, ALU.max))
            dve.wait_ge(setup_act_done, 1)
            step(nc.vector.tensor_scalar(SS2, EXPL, 2.0, None, ALU.add))
            step(nc.vector.reciprocal(SS1, SS2))
            step(nc.vector.tensor_tensor(SS1, SS1, EXPL, ALU.mult))
            step(nc.vector.tensor_tensor(SS2, SS1, SS1, ALU.mult))
            step(nc.vector.tensor_scalar(POLY, SS2, 1.0 / 13, 1.0 / 11, ALU.mult, ALU.add))
            for k in (9, 7, 5, 3, 1):
                step(nc.vector.tensor_tensor(POLY, POLY, SS2, ALU.mult))
                step(nc.vector.tensor_scalar(POLY, POLY, 1.0 / k, None, ALU.add))
            step(nc.vector.tensor_tensor(POLY, POLY, SS1, ALU.mult))
            step(nc.vector.tensor_scalar(SPT, NLAM, 0.0, None, ALU.max))
            step(nc.vector.scalar_tensor_tensor(SPT, POLY, 2.0, SPT, ALU.mult, ALU.add))
            step(nc.vector.tensor_scalar(col(C_M8, 8), SPT, -8.0, None, ALU.mult))
            step(nc.vector.tensor_scalar(col(C_P8, 8), SPT, 8.0, None, ALU.mult))

        def norm_reads_pe(pe):
            pe.wait_ge(rstd, 2)
            for t in range(TT):
                mm = nc.tensor.matmul(ps[:, 5, t:t + 1], rB[0:1, t * P:(t + 1) * P], ones[0:1, 0:1],
                                      start=True, stop=True)
            mm.then_inc(rcol_done, 1)

        def block_V(dst, c, k_ap, width, step):
            s = c % 2
            for k in range(KD):
                mm = three(dst, k_ap(xgh, k), k_ap(xgl, k), wh[:, s, k * step:k * step + width],
                           wl[:, s, k * step:k * step + width], k == 0, k == KD - 1)
            return mm

        BE = U_EVEN
        LAM_INIT = 0.8 - 0.6 * 1.0
        QS = 64 ** -0.5

        def rot_pe(pe, i):
            pe.wait_ge(q32_done, i + 1)
            if i >= 2:
                pe.wait_ge(qs_done, i - 1)
            nc.tensor.matmul(ps[:, 2 + i % 2, :], permA[:, :], q32[:, i % 2, :],
                             start=True, stop=True).then_inc(rot_done, 1)

        def diff_pe(pe):
            for i in range(18):
                if i < 16:
                    a, t, b = i // 4, i % 4, 2 * (i % 2)
                    if i >= 2:
                        pe.wait_ge(ea_done, 2 * (i - 1))
                    for m in range(2):
                        r = slice(64 * m, 64 * m + 64)
                        three(ps[:, b + m, :], qah[r, a, t * P:(t + 1) * P], qal[r, a, t * P:(t + 1) * P],
                              kah[r, a, :], kal[r, a, :], True, True).then_inc(sa_done, 1)
                j = i - 2
                if 0 <= j < 16:
                    a = j // 4
                    pe.wait_ge(al_done, j + 1)
                    if j >= 2:
                        pe.wait_ge(oa_done, j - 1)
                    for k in range(TT):
                        mm = three(ps[:, 6 + j % 2, 0:P], aTh[:, j % 2, k * P:(k + 1) * P],
                                   aTl[:, j % 2, k * P:(k + 1) * P], vah[:, k, a * P:(a + 1) * P],
                                   val[:, k, a * P:(a + 1) * P], k == 0, k == TT - 1)
                    mm.then_inc(pa_done, 1)
                j = i - 1
                if 0 <= j < 16:
                    pe.wait_ge(wa_done, j + 1)
                    if j >= 2:
                        pe.wait_ge(al_done, j - 1)
                    for k in range(TT):
                        mm = nc.tensor.transpose(ps[:, 4 + j % 2, k * P:(k + 1) * P],
                                                 eA[:, j % 2, 0, k * P:(k + 1) * P], ident[:, :])
                    mm.then_inc(ta_done, 1)

        def diff_act(act):
            for i in range(20):
                if i < 16:
                    act.wait_ge(mxa_done, i + 1)
                    if i >= 2:
                        act.wait_ge(ta_done, i - 1)
                    for m in range(2):
                        nc.scalar.activation(eA[:, i % 2, m, :], ps[:, 2 * (i % 2) + m, :], ACT.Exp,
                                             bias=col(C_NMX + 2 * (i % 2) + m),
                                             accum_out=col(C_SUM + 2 * (i % 2) + m)).then_inc(ea_done, 1)
                j = i - 1
                if 0 <= j < 16:
                    act.wait_ge(ta_done, j + 1)
                    if j >= 2:
                        act.wait_ge(pa_done, j - 1)
                    nc.scalar.activation(aTh[:, j % 2, :], ps[:, 4 + j % 2, :], ACT.Copy).then_inc(ah_done, 1)
                j = i - 4
                if 0 <= j < 16:
                    a, t = j // 4, j % 4
                    act.wait_ge(oa_done, j + 1)
                    if j:
                        act.wait_ge(ssa_done, j)
                    nc.scalar.activation(junk[:, :], oA[:, t, a * P:(a + 1) * P], ACT.Square,
                                         accum_out=col(C_SS + 4 * t + a)).then_inc(ssa_done, 1)
            act.wait_ge(ssa_done, 16)
            nc.scalar.activation(col(C_RS, 16), col(C_SS, 16), ACT.Sqrt, bias=col(C_EPS),
                                 scale=1.0 / P).then_inc(ssa_done, 1)

        def diff_dve(dve):
            for i in range(19):
                j = i - 1
                if 0 <= j < 16:
                    b = 2 * (j % 2)
                    dve.wait_ge(ea_done, 2 * j + 2)
                    nc.vector.reciprocal(col(C_REC + b, 2), col(C_SUM + b, 2)).then_inc(reca_done, 1)
                    dve.wait_ge(reca_done, 3 * j + 1)
                    nc.vector.tensor_tensor(col(C_CF + b), col(C_REC + b + 1), col(C_NLAM),
                                            ALU.mult).then_inc(reca_done, 1)
                    dve.wait_ge(reca_done, 3 * j + 2)
                    nc.vector.tensor_scalar(eA[:, j % 2, 1, :], eA[:, j % 2, 1, :], col(C_CF + b), None,
                                            ALU.mult).then_inc(reca_done, 1)
                    dve.wait_ge(reca_done, 3 * j + 3)
                    nc.vector.scalar_tensor_tensor(eA[:, j % 2, 0, :], eA[:, j % 2, 0, :], col(C_REC + b),
                                                   eA[:, j % 2, 1, :], ALU.mult, ALU.add).then_inc(wa_done, 1)
                if i < 16:
                    dve.wait_ge(sa_done, 2 * i + 2)
                    b = 2 * (i % 2)
                    nc.vector.tensor_reduce(col(C_NMX + b, 2), ps[:, b:b + 2, :], AX, ALU.max,
                                            negate=True).then_inc(mxa_done, 1)
                j = i - 3
                if 0 <= j < 16:
                    a, t = j // 4, j % 4
                    dve.wait_ge(pa_done, j + 1)
                    nc.vector.tensor_copy(oA[:, t, a * P:(a + 1) * P], ps[:, 6 + j % 2, 0:P]).then_inc(oa_done, 1)
                j = i - 1
                if 0 <= j < 16:
                    dve.wait_ge(ah_done, j + 1)
                    nc.vector.tensor_tensor(aTl[:, j % 2, :], ps[:, 4 + j % 2, :], aTh[:, j % 2, :].bitcast(F32),
                                            ALU.subtract).then_inc(al_done, 1)
            dve.wait_ge(ssa_done, 17)
            nc.vector.reciprocal(col(C_RS, 16), col(C_RS, 16)).then_inc(rsa_done, 1)
            dve.wait_ge(rsa_done, 1)
            dve.wait_ge(oa_done, 16)
            for t in range(TT):
                for a in range(4):
                    nc.vector.tensor_scalar(oA[:, t, a * P:(a + 1) * P], oA[:, t, a * P:(a + 1) * P],
                                            col(C_RS + 4 * t + a), None, ALU.mult).then_inc(oan_done, 1)

        def pair_of(kind, i):
            return (i // 4, i % 4) if kind == "N" else (i % 4, i // 4)

        def probs(kind, i, hh=None):
            t = pair_of(kind, i)[0]
            if kind == "M":
                buf, n, k0 = eD, 4, 0
            elif MTYPE[t] == 1:
                buf, n, k0 = p3, 3, t - 1
            else:
                buf, n, k0 = p3, 2, 2 * (t // 2)
            return (None if hh is None else buf[:, i % 2, hh, :]), n, k0

        def pair_pe(pe, kind, S):
            tTh, tTl, vh_, vl_ = (bTh, bTl, vbh, vbl) if kind == "N" else (dTh, dTl, vdh, vdl)
            for i in range(18):
                if i < 16:
                    t, hp = pair_of(kind, i)
                    if i >= 2:
                        pe.wait_ge(S["scores_read"], (1 if kind == "N" else 2) * (i - 1))
                    for hh in range(2):
                        dst = ps[:, 2 * (i % 2) + hh, :]
                        if kind == "N":
                            r, w = slice(64 * hh, 64 * hh + 64), WSTART[t]
                            dst = dst[:, 0:8 * WIN]
                            keys = [k[r, hp, :].rearrange("p (r c) -> p r c", r=GRID_R)[:, :, w:w + WIN]
                                    for k in (kbh, kbl)]
                            q = [k[r, hp, t * P:(t + 1) * P] for k in (qbh, qbl)]
                        else:
                            keys = [k[:, 2 * hp + hh, :] for k in (kdh, kdl)]
                            q = [k[:, 2 * hp + hh, t * P:(t + 1) * P] for k in (qdh, qdl)]
                        three(dst, *q, *keys, True, True).then_inc(S["scores"], 1)
                j = i - 1
                if 0 <= j < 16:
                    pe.wait_ge(S["exp"], 2 * j + 2)
                    if j:
                        pe.wait_ge(S["lo"], j)
                    for hh in range(2):
                        p, n, _ = probs(kind, j, hh)
                        for k in range(n):
                            mm = nc.tensor.transpose(ps[:, 4 + hh, k * P:(k + 1) * P],
                                                     p[:, k * P:(k + 1) * P], ident[:, :])
                    mm.then_inc(S["turned"], 1)
                j = i - 2
                if 0 <= j < 16:
                    t, hp = pair_of(kind, j)
                    _, n, k0 = probs(kind, j)
                    pe.wait_ge(S["lo"], j + 1)
                    if j >= 2:
                        pe.wait_ge(S["o"], j - 1)
                    for hh in range(2):
                        c = (2 * hp + hh) * 64
                        for k in range(n):
                            th_, tl_ = [x_[:, j % 2, hh, k * P:(k + 1) * P] for x_ in (tTh, tTl)]
                            mm = three(ps[:, 6 + j % 2, hh * 64:hh * 64 + 64], th_, tl_,
                                       vh_[:, k0 + k, c:c + 64], vl_[:, k0 + k, c:c + 64], k == 0, k == n - 1)
                    mm.then_inc(S["pv"], 1)

        def pair_act(act, kind, S):
            for i in range(17):
                if i < 16:
                    t, hp = pair_of(kind, i)
                    act.wait_ge(S["max"], i + 1)
                    if i >= 2:
                        act.wait_ge(S["turned"], i - 1)
                        act.wait_ge(S["rec"], i - 1)
                    for hh in range(2):
                        cc = 2 * (i % 2) + hh
                        if kind == "N":
                            p = probs(kind, i, hh)[0]
                            w = 64 if MTYPE[t] == 1 else 0
                            p = p[:, w:w + 8 * WIN]
                            if MTYPE[t] == 1:
                                act.wait_ge(p3_zero, 2)
                            nc.scalar.activation(p.rearrange("p (c j) -> p j c", j=8),
                                                 sB[:, i % 2, hh, :].rearrange("p (j c) -> p j c", j=8),
                                                 ACT.Exp, bias=col(C_NMX + cc),
                                                 accum_out=col(C_SUM + cc)).then_inc(S["exp"], 1)
                        else:
                            nc.scalar.activation(eD[:, i % 2, hh, :], ps[:, cc, :], ACT.Exp,
                                                 bias=col(C_NMX + cc), scale=MS,
                                                 accum_out=col(C_SUM + cc)).then_inc(S["exp"], 1)
                j = i - 1
                if 0 <= j < 16:
                    _, n, _ = probs(kind, j)
                    act.wait_ge(S["turned"], j + 1)
                    if j >= 2:
                        act.wait_ge(S["pv"], j - 1)
                    dst = (bTh if kind == "N" else dTh)[:, j % 2, :, 0:n * P]
                    nc.scalar.activation(dst, ps[:, 4:6, 0:n * P], ACT.Copy).then_inc(S["hi"], 1)

        def pair_dve(dve, kind, S):
            nred = 0
            for i in range(19):
                if i < 16:
                    t, hp = pair_of(kind, i)
                    b = 2 * (i % 2)
                    if kind == "N" and i % 4 == 0 and t != 2:
                        if i:
                            dve.wait_ge(S["scores_read"], i)
                        w0 = 47 - (WSTART[t] - 16 * t + 16)
                        rel = relb[:, :, ::-1, w0:(w0 - WIN if w0 >= WIN else None):-1]
                        mk = mask[:, MTYPE[t]:MTYPE[t] + 1, :].broadcast_to([P, 64, WIN])
                        nc.vector.tensor_tensor(bm[:, :, :, :], rel, mk.rearrange("p (h j) c -> p h j c", h=8),
                                                ALU.add).then_inc(bm_done, 1)
                        nred += 1
                        dve.wait_ge(bm_done, nred)
                    dve.wait_ge(S["scores"], 2 * i + 2)
                    if kind == "N":
                        if i >= 2:
                            dve.wait_ge(S["exp"], 2 * (i - 1))
                        nc.vector.tensor_tensor(sB[:, i % 2, :, :], ps[:, b:b + 2, 0:8 * WIN],
                                                bm[:, 2 * hp:2 * hp + 2, :, :].rearrange("p h j c -> p h (j c)"),
                                                ALU.add).then_inc(S["scores_read"], 1)
                        dve.wait_ge(S["scores_read"], i + 1)
                        nc.vector.tensor_reduce(col(C_NMX + b, 2), sB[:, i % 2, :, :], AX, ALU.max,
                                                negate=True).then_inc(S["max"], 1)
                    else:
                        nc.vector.tensor_reduce(col(C_CF + b, 2), ps[:, b:b + 2, :], AX, ALU.max).then_inc(mxraw, 1)
                        dve.wait_ge(mxraw, i + 1)
                        nc.vector.tensor_scalar(col(C_NMX + b, 2), col(C_CF + b, 2), -MS, None,
                                                ALU.mult).then_inc(S["max"], 1)
                j = i - 1
                if 0 <= j < 16:
                    dve.wait_ge(S["exp"], 2 * j + 2)
                    if j >= 4:
                        dve.wait_ge(S["o"], j - 3)
                    nc.vector.reciprocal(recs[:, 2 * (j % 4):2 * (j % 4) + 2],
                                         col(C_SUM + 2 * (j % 2), 2)).then_inc(S["rec"], 1)
                if kind == "N" and i == 4:
                    dve.wait_ge(S["turned"], 4)
                    for z in (slice(0, 64), slice(320, 384)):
                        nc.vector.memset(p3[:, :, :, z], 0.0).then_inc(p3_zero, 1)
                j = i - 3
                if 0 <= j < 16:
                    t, hp = pair_of(kind, j)
                    o_ = (oB if kind == "N" else oD)[:, t, hp * P:(hp + 1) * P]
                    dve.wait_ge(S["pv"], j + 1)
                    dve.wait_ge(S["rec"], j + 1)
                    rec = recs[:, 2 * (j % 4):2 * (j % 4) + 2]
                    nc.vector.tensor_tensor(o_.rearrange("p (h e) -> p h e", h=2),
                                            ps[:, 6 + j % 2, 0:P].rearrange("p (h e) -> p h e", h=2),
                                            rec.unsqueeze(2).broadcast_to([P, 2, 64]), ALU.mult).then_inc(S["o"], 1)
                j = i - 1
                if 0 <= j < 16:
                    _, n, _ = probs(kind, j)
                    dst, hi = ((bTl, bTh) if kind == "N" else (dTl, dTh))
                    dst, hi = dst[:, j % 2, :, 0:n * P], hi[:, j % 2, :, 0:n * P]
                    dve.wait_ge(S["hi"], j + 1)
                    nc.vector.tensor_tensor(dst, ps[:, 4:6, 0:n * P], hi.bitcast(F32),
                                            ALU.subtract).then_inc(S["lo"], 1)

        def turn_pe(pe, src, tiles, gate, reads):
            for n, (k, f) in enumerate(tiles):
                if n == 0:
                    for g in gate:
                        pe.wait_ge(*g)
                for t in range(TT):
                    mm = nc.tensor.transpose(ps[:, k % 4, t * P:(t + 1) * P], src[:, t, f * P:(f + 1) * P],
                                             ident[:, :])
                mm.then_inc(reads, 1)

        def down_mixer_pe(pe, B, split_done):
            for j in range(3):
                c = B + j
                s = c % 2
                pe.wait_ge(w_lo, c + 1)
                pe.wait_ge(split_done, 8)
                for k2 in range(2):
                    for b in (4, 5, 6, 7, 0, 1, 2, 3):
                        o = k2 * D + b * P
                        mm = three(ps[:, b, :], wh[:, s, o:o + P], wl[:, s, o:o + P],
                                   xgh[:, 2 * j + k2, :], xgl[:, 2 * j + k2, :], j == 0 and k2 == 0, False)
                    mm.then_inc(w_half, 1)
            down_last_pe(pe, B + 3, 6, xgh, xgl)

        def even_load(act):
            act.wait_ge(x_new, 8)
            for dst, src in ((cosA, rope_a[0:P, :]), (sinA, rope_a[P:2 * P, :]), (permA, perm_d[:, 0:P])):
                act.dma_start(dst[:, :], src).then_inc(even_in, 16)
            act.dma_start(lamb, lamvec.partition_broadcast(P)).then_inc(even_in, 16)

        def even_load_bias(pool):
            pool.wait_ge(ssum_done, 2)
            pool.dma_start(mask, masks_d.rearrange("p (m c) -> p m c", m=3)).then_inc(mask_in, 16)
            for h in range(8):
                for j in range(8):
                    src = bass.AP(tensor=rpb.tensor, offset=960 * h + 64 * j, ap=[[1, 16], [64, 8], [1, 48]])
                    pool.dma_start(relb[:, h, j, :], src).then_inc(mask_in, 16)

        def even_pe(pe):
            for i in range(8):
                c = BE + i // 2
                pe.wait_ge(w_lo, c + 1)
                if i >= 2:
                    pe.wait_ge(q32_done, i - 1)
                block_T(pe, ps[:, i % 2, :], c, i % 2, wait_x=8 if i == 0 else None).then_inc(w_half, 1)
                if i == 0:
                    norm_pe(pe, 1, 4)
                    pe.wait_ge(even_in, 64)
                else:
                    rot_pe(pe, i - 1)
                if i == 1:
                    norm_reads_pe(pe)
            for v in range(2):
                c = BE + 4 + v
                pe.wait_ge(w_lo, c + 1)
                for t in range(TT):
                    if v == 0 and t == 0:
                        pe.wait_ge(rcol_read, 1)
                    if v == 1:
                        pe.wait_ge(va_lo, t + 1)
                    mm = block_V(ps[:, 4 + t, 0:256], c, lambda b, k, t=t: b[:, k, t * P:(t + 1) * P], 256, 256)
                    if t % 2:
                        mm.then_inc(w_half, 1)
                    if v == 0 and t == 0:
                        rot_pe(pe, 7)
            pe.wait_ge(qa_lo, 8)
            pe.wait_ge(va_lo, 8)
            diff_pe(pe)
            for i in range(13):
                if i < 12:
                    c = BE + 6 + i // 2
                    pe.wait_ge(w_lo, c + 1)
                    if i >= 2:
                        pe.wait_ge(qb32_done, i - 1)
                    block_T(pe, ps[:, i % 2, :], c, i % 2).then_inc(w_half, 1)
                j = i - 1
                if j >= 8:
                    pe.wait_ge(qb32_done, j + 1)
                    if j >= 10:
                        pe.wait_ge(vb_lo, j - 9)
                    for t in range(TT):
                        mm = nc.tensor.transpose(ps[:, 2 + j % 2, t * P:(t + 1) * P],
                                                 qb32[:, j % 2, t * P:(t + 1) * P], ident[:, :])
                    mm.then_inc(vt_done, 1)
            pe.wait_ge(qb_lo, 8)
            pe.wait_ge(vb_lo, 4)
            pe.wait_ge(oa_done, 16)
            pair_pe(pe, "N", SN)
            turn_pe(pe, oA, [(k, k) for k in range(4)], [(oan_done, 16)], mt_done)
            for k in range(4):
                if k == 0:
                    pe.wait_ge(SN["o"], 16)
                pe.wait_ge(mix_lo, k + 1)
                for t in range(TT):
                    mm = nc.tensor.transpose(ps[:, k, t * P:(t + 1) * P], oB[:, t, k * P:(k + 1) * P], ident[:, :])
                mm.then_inc(mt_done, 1)
            down_mixer_pe(pe, BE + 12, mix_lo)

        def even_act(act):
            even_load(act)
            for i in range(8):
                c = BE + i // 2
                if i % 2 == 0:
                    split_hi(act, c + 1)
                if i == 0:
                    norm_act(act, 1, 4)
                    act.wait_ge(even_in, 64)
                if i == 1:
                    act.wait_ge(lam_done, 2)
                    nc.scalar.activation(col(C_LAM, 2), col(C_LAM, 2), ACT.Exp).then_inc(lam_exp, 1)
                if i >= 1:
                    qa_hi_act(act, i - 1)
            split_hi(act, BE + 5)
            qa_hi_act(act, 7)
            for v in range(2):
                c = BE + 4 + v
                if v:
                    split_hi(act, c + 1)
                for t in range(TT):
                    act.wait_ge(w_half, 2 * c + t // 2 + 1)
                    act.wait_ge(rcol_read, 1)
                    nc.scalar.activation(vah[:, t, v * 256:v * 256 + 256], ps[:, 4 + t, 0:256], ACT.Copy,
                                         scale=col(C_RN + t)).then_inc(va_hi, 1)
            diff_act(act)
            for i in range(12):
                c = BE + 6 + i // 2
                if i % 2 == 0:
                    split_hi(act, c + 1)
                if i < 8:
                    dst = (qbh if i < 4 else kbh)[:, i % 4, :]
                    act.wait_ge(qb32_done, i + 1)
                    nc.scalar.activation(dst, qb32[:, i % 2, :], ACT.Copy).then_inc(qb_hi, 1)
                else:
                    f = i - 8
                    act.wait_ge(vt_done, f + 1)
                    nc.scalar.activation(vbh[:, :, f * P:(f + 1) * P],
                                         ps[:, 2 + i % 2, :].rearrange("p (t f) -> p t f", t=TT),
                                         ACT.Copy).then_inc(vb_hi, 1)
            pair_act(act, "N", SN)
            for k in range(8):
                act.wait_ge(mt_done, k + 1)
                if k < 4:
                    nc.scalar.activation(xgh[:, k, :], ps[:, k, :], ACT.Copy, scale=vec(V_SUB)).then_inc(mix_hi, 1)
                else:
                    nc.scalar.activation(xgh[:, k, :].rearrange("p (r c) -> p c r", r=GRID_R),
                                         ps[:, k - 4, :].rearrange("p (c r) -> p c r", r=GRID_R),
                                         ACT.Copy).then_inc(mix_hi, 1)
            for j in range(4):
                split_hi(act, BE + 13 + j)
            finish_act(act, 2, BE + 15)

        def qa_hi_act(act, i):
            dst = (qah if i < 4 else kah)[:, i % 4, :]
            act.wait_ge(qr_done, i + 1)
            nc.scalar.activation(dst, qs[:, i % 2, :], ACT.Copy, scale=QS if i < 4 else 1.0).then_inc(qa_hi, 1)

        def even_dve(dve):
            dve.wait_ge(even_in, 64)
            nc.vector.tensor_tensor(lamp, lamb.rearrange("p (a b e) -> p a b e", a=2, b=2)[:, :, 0, :],
                                    lamb.rearrange("p (a b e) -> p a b e", a=2, b=2)[:, :, 1, :],
                                    ALU.mult).then_inc(lam_done, 1)
            dve.wait_ge(lam_done, 1)
            nc.vector.tensor_reduce(col(C_LAM, 2), lamp, AX, ALU.add).then_inc(lam_done, 1)
            for i in range(8):
                c = BE + i // 2
                if i % 2 == 0:
                    split_lo(dve, c + 1)
                if i == 0:
                    norm_dve(dve, 1)
                    dve.wait_ge(rstd, 2)
                dve.wait_ge(w_half, 2 * c + i % 2 + 1)
                if i >= 2:
                    dve.wait_ge(qc_done, i - 1)
                nc.vector.tensor_tensor(q32[:, i % 2, :], ps[:, i % 2, :], rB[:, :], ALU.mult).then_inc(q32_done, 1)
                if i >= 1:
                    qa_dve(dve, i - 1)
                if i == 3:
                    dve.wait_ge(lam_exp, 1)
                    nc.vector.scalar_tensor_tensor(col(C_NLAM), col(C_LAM + 1), -LAM_INIT, col(C_LAM),
                                                   ALU.add, ALU.subtract).then_inc(lam_done, 1)
                    nc.vector.tensor_scalar(vec(V_SUB), vec(V_SUB), 1.0 - LAM_INIT, None,
                                            ALU.mult).then_inc(lam_done, 1)
                    dve.wait_ge(rcol_done, 1)
                    nc.vector.tensor_copy(col(C_RN, 4), ps[:, 5, 0:4]).then_inc(rcol_read, 1)
            split_lo(dve, BE + 5)
            qa_dve(dve, 7)
            for v in range(2):
                c = BE + 4 + v
                if v:
                    split_lo(dve, c + 1)
                for t in range(TT):
                    dve.wait_ge(va_hi, 4 * v + t + 1)
                    nc.vector.scalar_tensor_tensor(val[:, t, v * 256:v * 256 + 256], ps[:, 4 + t, 0:256],
                                                   col(C_RN + t), vah[:, t, v * 256:v * 256 + 256].bitcast(F32),
                                                   ALU.mult, ALU.subtract).then_inc(va_lo, 1)
            dve.wait_ge(lam_done, 4)
            diff_dve(dve)
            for i in range(12):
                c = BE + 6 + i // 2
                if i % 2 == 0:
                    split_lo(dve, c + 1)
                dve.wait_ge(w_half, 2 * c + i % 2 + 1)
                if 2 <= i < 10:
                    dve.wait_ge(qb_lo, i - 1)
                elif i >= 10:
                    dve.wait_ge(vt_done, i - 9)
                if i < 4 or i >= 8:
                    nc.vector.scalar_tensor_tensor(qb32[:, i % 2, :].rearrange("p (c r) -> p r c", r=GRID_R),
                                                   ps[:, i % 2, :].rearrange("p (r c) -> p r c", r=GRID_R),
                                                   QS if i < 4 else 1.0,
                                                   rB[:, :].rearrange("p (r c) -> p r c", r=GRID_R),
                                                   ALU.mult, ALU.mult).then_inc(qb32_done, 1)
                else:
                    nc.vector.tensor_tensor(qb32[:, i % 2, :], ps[:, i % 2, :], rB[:, :],
                                            ALU.mult).then_inc(qb32_done, 1)
                if i < 8:
                    dve.wait_ge(qb_hi, i + 1)
                    hi, lo = (t_[:, i % 4, :] for t_ in ((qbh, qbl) if i < 4 else (kbh, kbl)))
                    nc.vector.tensor_tensor(lo, qb32[:, i % 2, :], hi.bitcast(F32), ALU.subtract).then_inc(qb_lo, 1)
                if i >= 9:
                    vb_lo_dve(dve, i - 1)
            vb_lo_dve(dve, 11)
            dve.wait_ge(mask_in, 65 * 16)
            pair_dve(dve, "N", SN)
            for k in range(8):
                dve.wait_ge(mix_hi, k + 1)
                if k < 4:
                    nc.vector.scalar_tensor_tensor(xgl[:, k, :], ps[:, k, :], vec(V_SUB), xgh[:, k, :].bitcast(F32),
                                                   ALU.mult, ALU.subtract).then_inc(mix_lo, 1)
                else:
                    nc.vector.tensor_tensor(xgl[:, k, :].rearrange("p (r c) -> p c r", r=GRID_R),
                                            ps[:, k - 4, :].rearrange("p (c r) -> p c r", r=GRID_R),
                                            xgh[:, k, :].bitcast(F32).rearrange("p (r c) -> p c r", r=GRID_R),
                                            ALU.subtract).then_inc(mix_lo, 1)
            for j in range(4):
                split_lo(dve, BE + 13 + j)
            finish_dve(dve, 2, 1.0, BE + 15)

        def vb_lo_dve(dve, i):
            f = i - 8
            dve.wait_ge(vb_hi, f + 1)
            nc.vector.tensor_tensor(vbl[:, :, f * P:(f + 1) * P],
                                    ps[:, 2 + i % 2, :].rearrange("p (t f) -> p t f", t=TT),
                                    vbh[:, :, f * P:(f + 1) * P].bitcast(F32), ALU.subtract).then_inc(vb_lo, 1)

        def qa_dve(dve, i):
            dve.wait_ge(rot_done, i + 1)
            if i >= 2:
                dve.wait_ge(qa_lo, i - 1)
            nc.vector.tensor_tensor(qs[:, i % 2, :], ps[:, 2 + i % 2, :], sinA[:, :], ALU.mult).then_inc(qs_done, 1)
            dve.wait_ge(qc_done, i + 1)
            dve.wait_ge(qs_done, i + 1)
            nc.vector.tensor_tensor(qs[:, i % 2, :], qs[:, i % 2, :], qc[:, i % 2, :], ALU.add).then_inc(qr_done, 1)
            dve.wait_ge(qa_hi, i + 1)
            hi, lo = (t_[:, i % 4, :] for t_ in ((qah, qal) if i < 4 else (kah, kal)))
            nc.vector.scalar_tensor_tensor(lo, qs[:, i % 2, :], QS if i < 4 else 1.0, hi.bitcast(F32),
                                           ALU.mult, ALU.subtract).then_inc(qa_lo, 1)

        def even_pool(pool):
            pool.wait_ge(even_in, 64)
            for i in range(8):
                pool.wait_ge(q32_done, i + 1)
                if i >= 2:
                    pool.wait_ge(qr_done, i - 1)
                nc.gpsimd.tensor_tensor(qc[:, i % 2, :], q32[:, i % 2, :], cosA[:, :], ALU.mult).then_inc(qc_done, 1)
            even_load_bias(pool)
            finish_pool(pool, 2)

        BO = U_ODD
        MS = 96 ** -0.5
        INB = ([(BO + i // 2, i % 2, P) for i in range(4)] + [(BO + 2, 0, P), (BO + 2, 1, P), (BO + 3, 0, P),
               (BO + 3, 1, 96)] + [(BO + 5 + i // 2, i % 2, P) for i in range(4)])
        N_IN = len(INB)
        U_GATE, U_UQ, U_UKV, U_WO = BO + 4, BO + 7, BO + 8, BO + 9

        def odd_block_pe(pe, i):
            c, m, rows = INB[i]
            pe.wait_ge(w_lo, c + 1)
            if i >= 4:
                pe.wait_ge(in_read, i - 3)
            if i in (8, 9):
                pe.wait_ge(cstd_done, i - 7)
            block_T(pe, ps[0:rows, i % 4, :], c, m, width=rows,
                    wait_x=32 if i == 0 else None).then_inc(w_half, 1)

        def odd_pe(pe):
            odd_block_pe(pe, 0)
            norm_pe(pe, 4, 4)
            for i in range(1, 8):
                odd_block_pe(pe, i)
            pe.wait_ge(csq_sum, 1)
            pe.wait_ge(in_read, 6)
            pe.wait_ge(std_done, 5)
            nc.tensor.matmul(ps[:, 0, :], ones[:, :], sqt[:, 1, :], start=True, stop=True).then_inc(cs_done, 1)
            pe.wait_ge(csq_done, 3)
            nc.tensor.matmul(ps[:, 1, :], ones[:, :], acc[:, :], start=True, stop=True).then_inc(cs_done, 1)
            pe.wait_ge(w_lo, U_GATE + 1)
            s = U_GATE % 2
            for g in range(8):
                c, d = g // 2, g % 2
                if d == 0:
                    pe.wait_ge(u_lo, c + 1)
                if g >= 2:
                    pe.wait_ge(sig_done, 2 * (g - 1))
                for kind in range(2):
                    o = (d * 8 + kind * 4 + c) * P
                    mm = three(ps[:, 4 + 2 * (g % 2) + kind, :], wh[:, s, o:o + P], wl[:, s, o:o + P],
                               uh[:, c, :], ul[:, c, :], True, True)
                    if g < 7 or kind == 0:
                        mm.then_inc(gate_done, 1)
                    else:
                        mm.then_inc(w_half, 2)
            for i in range(8, N_IN):
                odd_block_pe(pe, i)
            pe.wait_ge(odd_in, 48)
            pe.wait_ge(w_lo, U_UKV + 1)
            pe.wait_ge(cq_lo, 3)
            pe.wait_ge(in_read, N_IN)
            pe.wait_ge(sig_done, 16)
            sq, sk = U_UQ % 2, U_UKV % 2
            rotd_pe(pe, 0)
            for h in range(8):
                if h >= 2:
                    pe.wait_ge(qd32_done, h)
                for k in range(2):
                    o = k * 768 + h * 96
                    mm = three(ps[0:96, h % 2, :], wh[:, sq, o:o + 96], wl[:, sq, o:o + 96],
                               cqh[:, k, :], cql[:, k, :], k == 0, k == 1)
                mm.then_inc(*((qd_ps, 1) if h < 7 else (w_half, 2)))
                if h >= 2:
                    pe.wait_ge(kd_lo, h - 1)
                three(ps[:, 4 + h % 2, :], wh[:, sk, h * P:(h + 1) * P], wl[:, sk, h * P:(h + 1) * P],
                      cqh[:, 2, :], cql[:, 2, :], True, True).then_inc(kd_ps, 1)
                rotd_pe(pe, h + 1)
                t = h - 4
                if t >= 0:
                    if t >= 2:
                        pe.wait_ge(vd_lo, t - 1)
                    wv = [w_[:, sk, 0:1024].rearrange("p (h e) -> p h e", h=8)[:, :, 64:128] for w_ in (wh, wl)]
                    mm = three(ps[:, 6 + t % 2, :], cqh[:, 2, t * P:(t + 1) * P], cql[:, 2, t * P:(t + 1) * P],
                               *wv, True, True)
                    mm.then_inc(*((vd_ps, 1) if t < 3 else (w_half, 2)))
            pe.wait_ge(vd_lo, 4)
            pe.wait_ge(qd_lo, 9)
            pe.wait_ge(kd_lo, 8)
            pair_pe(pe, "M", SM)
            for k in range(4):
                if k == 0:
                    pe.wait_ge(SM["o"], 16)
                for t in range(TT):
                    mm = nc.tensor.transpose(ps[:, k, t * P:(t + 1) * P], oD[:, t, k * P:(k + 1) * P], ident[:, :])
                mm.then_inc(omt_done, 1)
            down_mixer_pe(pe, U_WO, omix_lo)

        def rotd_pe(pe, i):
            pe.wait_ge(qd32_done, i + 1)
            if i >= 2:
                pe.wait_ge(qds_done, i - 1)
            nc.tensor.matmul(ps[0:96, 2 + i % 2, :], permD[:, :], qd32[:, i % 2, :],
                             start=True, stop=True).then_inc(rotd_done, 1)

        def odd_act(act):
            def u_hi_act(k):
                act.wait_ge(u_done, 4 * k + 4)
                nc.scalar.activation(uh[:, k, :], u32[:, k, :], ACT.Copy).then_inc(u_hi, 1)

            split_hi(act, BO + 1)
            norm_act(act, 4, 4)
            split_hi(act, BO + 2)
            split_hi(act, BO + 3)
            u_hi_act(0)
            split_hi(act, U_GATE)
            u_hi_act(1)
            u_hi_act(2)
            act.wait_ge(in_read, 7)
            act.wait_ge(std_done, 5)
            act.wait_ge(rstd, 5)
            act.wait_ge(ssum_done, 5)
            nc.scalar.activation(sqt[:, 0, :], cq[:, 0, :], ACT.Square).then_inc(csq_done, 1)
            nc.scalar.activation(sqt[:, 1, :], cq[:, 1, :], ACT.Square).then_inc(csq_done, 1)
            nc.scalar.activation(acc[:, :], cq[:, 2, :], ACT.Square).then_inc(csq_done, 1)
            split_hi(act, U_GATE + 1)
            for z, n in enumerate((256, 128)):
                act.wait_ge(cs_done, 2)
                nc.scalar.activation(sqt[:, z, :], ps[:, z, :], ACT.Sqrt, bias=col(C_EPS),
                                     scale=1.0 / n).then_inc(cstd_done, 1)
            u_hi_act(3)
            for g in range(8):
                c, d = g // 2, g % 2
                for kind in range(2):
                    act.wait_ge(gate_done, 2 * g + kind + 1) if (g, kind) != (7, 1) else                         act.wait_ge(w_half, 2 * (U_GATE + 1))
                    dst = (ra, iu)[kind][:, g, :]
                    nc.scalar.activation(dst, ps[:, 4 + 2 * (g % 2) + kind, :], ACT.Sigmoid,
                                         bias=vec((V_BA, V_BX)[kind] + 4 * d + c)).then_inc(sig_done, 1)
            split_hi(act, U_GATE + 2)
            for g in range(8):
                c, d = g // 2, g % 2
                act.wait_ge(sig_done, 2 * g + 1)
                nc.scalar.activation(th[:, g, :], ra[:, g, :], ACT.Tanh, scale=col(C_P8 + 4 * d + c)).then_inc(th_done, 1)
            for g in range(8):
                c, d = g // 2, g % 2
                act.wait_ge(th_done, g + 1)
                nc.scalar.activation(ra[:, g, :], ra[:, g, :], ACT.Exp, scale=col(C_M8 + 4 * d + c)).then_inc(a_done, 1)
            for k in range(3):
                act.wait_ge(cqn_done, k + 1)
                nc.scalar.activation(cqh[:, k, :], cq[:, k, :], ACT.Copy).then_inc(cq_hi, 1)
            for g in range(8):
                act.wait_ge(vv_done, g + 1)
                nc.scalar.activation(th[:, g, :], th[:, g, :], ACT.Sqrt).then_inc(mult_done, 1)
            split_hi(act, U_UQ)
            for c in range(4):
                act.wait_ge(in_read, 9 + c)
                nc.scalar.activation(gc[:, c, :], gc[:, c, :], ACT.Gelu_apprx_tanh).then_inc(gelu_done, 1)
            split_hi(act, U_UKV)
            for c in range(4):
                act.wait_ge(oc_done, c + 1)
                nc.scalar.activation(xgh[:, c, :], gc[:, c, :], ACT.Copy).then_inc(omix_hi, 1)
            for i in range(10):
                if i == 0:
                    act.wait_ge(omix_lo, 4)
                    nc.scalar.activation(qd32[:, 0, :], kpe[:, :], ACT.Copy).then_inc(qd32_done, 1)
                elif i < 9:
                    act.wait_ge(qd_ps, i) if i < 8 else act.wait_ge(w_half, 2 * (U_UQ + 1))
                    if i >= 2:
                        act.wait_ge(qdc_done, i - 1)
                        act.wait_ge(rotd_done, i - 1)
                    nc.scalar.activation(qd32[:, i % 2, :], ps[0:96, (i - 1) % 2, :], ACT.Copy).then_inc(qd32_done, 1)
                h = i - 1
                if 0 <= h < 8:
                    act.wait_ge(kd_ps, h + 1)
                    nc.scalar.activation(kdh[0:64, h, :], ps[0:64, 4 + h % 2, :], ACT.Copy).then_inc(kd_hi, 1)
                if i >= 1:
                    qd_hi_act(act, i - 1)
                t = i - 5
                if 0 <= t < 4:
                    act.wait_ge(vd_ps, t + 1) if t < 3 else act.wait_ge(w_half, 2 * (U_UKV + 1))
                    nc.scalar.activation(vdh[:, t, :], ps[:, 6 + t % 2, :], ACT.Copy).then_inc(vd_hi, 1)
            split_hi(act, U_WO)
            pair_act(act, "M", SM)
            for k in range(4):
                act.wait_ge(omt_done, k + 1)
                nc.scalar.activation(xgh[:, 4 + k, :], ps[:, k, :], ACT.Copy).then_inc(omix_hi, 1)
            for j in range(4):
                split_hi(act, U_WO + 1 + j)
            finish_act(act, 5, U_WO + 3)

        def qd_hi_act(act, i):
            act.wait_ge(qdr_done, i + 1)
            if i:
                nc.scalar.activation(qdh[:, i - 1, :], qds[:, i % 2, :], ACT.Copy).then_inc(qd_hi, 1)
            else:
                nc.scalar.activation(kdh[64:96, :, :], qds[64:96, 0:1, :].broadcast_to([32, 8, SEQ]),
                                     ACT.Copy).then_inc(qd_hi, 1)

        def odd_dve(dve):
            def evac(i):
                c, m, rows = INB[i]
                dst = (xcp[:, i, 1:SEQ + 1] if i < 4 else cq[:, i - 4, :] if i < 7 else kpe[:, :] if i == 7
                       else gc[:, i - 8, :])
                dve.wait_ge(w_half, 2 * c + m + 1)
                nc.vector.tensor_tensor(dst, ps[0:rows, i % 4, :], rB[0:rows, :], ALU.mult).then_inc(in_read, 1)

            def u_lo_dve(k):
                dve.wait_ge(u_hi, k + 1)
                nc.vector.tensor_tensor(ul[:, k, :], u32[:, k, :], uh[:, k, :].bitcast(F32),
                                        ALU.subtract).then_inc(u_lo, 1)

            split_lo(dve, BO + 1)
            nc.vector.memset(xcp[:, :, 0:1], 0.0).then_inc(pad_done, 1)
            nc.vector.memset(xcp[:, :, SEQ + 1:SEQ + 3], 0.0).then_inc(pad_done, 1)
            norm_dve(dve, 4)
            dve.wait_ge(rstd, 5)
            evac(0)
            evac(1)
            split_lo(dve, BO + 2)
            evac(2)
            evac(3)
            for i in range(4, 8):
                if i % 2 == 0:
                    split_lo(dve, BO + i // 2 + 1)
                evac(i)
                conv_dve(dve, i - 4)
                if i > 4:
                    u_lo_dve(i - 5)
            split_lo(dve, U_GATE + 1)
            u_lo_dve(3)
            for z in range(2):
                dve.wait_ge(cstd_done, z + 1)
                nc.vector.reciprocal(sqt[:, z, :], sqt[:, z, :]).then_inc(crs_done, 1)
            for k in range(3):
                dve.wait_ge(crs_done, k // 2 + 1)
                nc.vector.scalar_tensor_tensor(cq[:, k, :], cq[:, k, :], vec(V_GQ + k), sqt[:, k // 2, :],
                                               ALU.mult, ALU.mult).then_inc(cqn_done, 1)
            split_lo(dve, U_GATE + 2)
            evac(8)
            evac(9)
            for g in range(8):
                dve.wait_ge(th_done, g + 1)
                nc.vector.tensor_scalar(th[:, g, :], th[:, g, :], 2.0 ** -115, None, ALU.max).then_inc(tmax_done, 1)
                if g % 2:
                    dve.wait_ge(a_done, g + 1)
                    if g >= 4:
                        dve.wait_ge(vv_done, g - 3)
                    nc.vector.tensor_tensor(sq_of(g), ra[:, g, :], ra[:, g, :], ALU.mult).then_inc(asqo_done, 1)
                    dve.wait_ge(asqo_done, g // 2 + 1)
                else:
                    dve.wait_ge(asq_done, g // 2 + 1)
                dve.wait_ge(tmax_done, g + 1)
                nc.vector.scalar_tensor_tensor(th[:, g, :], sq_of(g), 1.0, th[:, g, :],
                                               ALU.add, ALU.mult).then_inc(vv_done, 1)
            evac(10)
            for k in range(3):
                dve.wait_ge(cq_hi, k + 1)
                nc.vector.tensor_tensor(cql[:, k, :], cq[:, k, :], cqh[:, k, :].bitcast(F32),
                                        ALU.subtract).then_inc(cq_lo, 1)
            evac(11)
            split_lo(dve, U_UQ)
            for g in range(8):
                c, d = g // 2, g % 2
                first = SEQ - 1 if d else 0
                dve.wait_ge(mult_done, g + 1)
                nc.vector.memset(th[:, g, first:first + 1], 1.0).then_inc(one_done, 1)
                dve.wait_ge(iu_done, g + 1)
                dve.wait_ge(one_done, g + 1)
                nc.vector.tensor_tensor(iu[:, g, :], iu[:, g, :], th[:, g, :], ALU.mult).then_inc(bt_done, 1)
                dve.wait_ge(bt_done, g + 1)
                rev = slice(None, None, -1) if d else slice(None)
                nc.vector.tensor_tensor_scan(th[:, g, rev], ra[:, g, rev], iu[:, g, rev], 0.0,
                                             ALU.mult, ALU.add).then_inc(h_done, 1)
                if d:
                    dve.wait_ge(h_done, g + 1)
                    nc.vector.tensor_tensor(th[:, g, :], th[:, g, :], th[:, g - 1, :], ALU.add).then_inc(hs_done, 1)
                    dve.wait_ge(hs_done, c + 1)
                    dve.wait_ge(gelu_done, c + 1)
                    nc.vector.tensor_tensor(gc[:, c, :], gc[:, c, :], th[:, g, :], ALU.mult).then_inc(oc_done, 1)
                    if c == 0:
                        split_lo(dve, U_UKV)
                    dve.wait_ge(omix_hi, c + 1)
                    nc.vector.tensor_tensor(xgl[:, c, :], gc[:, c, :], xgh[:, c, :].bitcast(F32),
                                            ALU.subtract).then_inc(omix_lo, 1)
            def vd_lo_dve(t):
                dve.wait_ge(vd_hi, t + 1)
                nc.vector.tensor_tensor(vdl[:, t, :], ps[:, 6 + t % 2, :], vdh[:, t, :].bitcast(F32),
                                        ALU.subtract).then_inc(vd_lo, 1)

            for i in range(9):
                dve.wait_ge(odd_in, 48)
                dve.wait_ge(rotd_done, i + 1)
                if i >= 2:
                    dve.wait_ge(qd_lo, i - 1)
                nc.vector.tensor_tensor(qds[:, i % 2, :], ps[0:96, 2 + i % 2, :], sinD[:, :],
                                        ALU.mult).then_inc(qds_done, 1)
                dve.wait_ge(qdc_done, i + 1)
                dve.wait_ge(qds_done, i + 1)
                nc.vector.tensor_tensor(qds[:, i % 2, :], qds[:, i % 2, :], qdc[:, i % 2, :],
                                        ALU.add).then_inc(qdr_done, 1)
                h = i - 1
                if h >= 0:
                    dve.wait_ge(kd_hi, h + 1)
                    nc.vector.tensor_tensor(kdl[0:64, h, :], ps[0:64, 4 + h % 2, :], kdh[0:64, h, :].bitcast(F32),
                                            ALU.subtract).then_inc(kd_lo, 1)
                t = i - 6
                if t >= 0:
                    vd_lo_dve(t)
                dve.wait_ge(qd_hi, i + 1)
                if i:
                    nc.vector.tensor_tensor(qdl[:, i - 1, :], qds[:, i % 2, :], qdh[:, i - 1, :].bitcast(F32),
                                            ALU.subtract).then_inc(qd_lo, 1)
                else:
                    nc.vector.tensor_tensor(kdl[64:96, :, :], qds[64:96, 0:1, :].broadcast_to([32, 8, SEQ]),
                                            kdh[64:96, :, :].bitcast(F32), ALU.subtract).then_inc(qd_lo, 1)
            vd_lo_dve(3)
            split_lo(dve, U_WO)
            pair_dve(dve, "M", SM)
            for k in range(4):
                dve.wait_ge(omix_hi, 4 + k + 1)
                nc.vector.tensor_tensor(xgl[:, 4 + k, :], ps[:, k, :], xgh[:, 4 + k, :].bitcast(F32),
                                        ALU.subtract).then_inc(omix_lo, 1)
            for j in range(4):
                split_lo(dve, U_WO + 1 + j)
            finish_dve(dve, 5, 1.0, U_WO + 3)

        def sq_of(g):
            return xcp[:, g % 4, 0:SEQ]

        def conv_dve(dve, k):
            dve.wait_ge(in_read, k + 1)
            dve.wait_ge(pad_done, 2)
            for j in range(4):
                if j == 0:
                    ins = nc.vector.tensor_scalar(u32[:, k, :], xcp[:, k, 0:SEQ], vec(V_CW + k), vec(V_CB + k),
                                                  ALU.mult, ALU.add)
                else:
                    dve.wait_ge(u_done, 4 * k + j)
                    ins = nc.vector.scalar_tensor_tensor(u32[:, k, :], xcp[:, k, j:j + SEQ], vec(V_CW + 4 * j + k),
                                                         u32[:, k, :], ALU.mult, ALU.add)
                ins.then_inc(u_done, 1)

        def odd_pool(pool):
            pool.wait_ge(csq_done, 2)
            nc.gpsimd.tensor_tensor(sqt[:, 1, :], sqt[:, 0, :], sqt[:, 1, :], ALU.add).then_inc(csq_sum, 1)
            for g in range(8):
                pool.wait_ge(sig_done, 2 * g + 2)
                nc.gpsimd.tensor_tensor(iu[:, g, :], iu[:, g, :], u32[:, g // 2, :], ALU.mult).then_inc(iu_done, 1)
            for g in range(0, 8, 2):
                pool.wait_ge(a_done, g + 1)
                if g >= 4:
                    pool.wait_ge(vv_done, g - 3)
                nc.gpsimd.tensor_tensor(sq_of(g), ra[:, g, :], ra[:, g, :], ALU.mult).then_inc(asq_done, 1)
            pool.wait_ge(omix_lo, 4)
            for dst, src in ((cosD, rope_d[0:96, :]), (sinD, rope_d[96:192, :]), (permD, perm_d[0:96, P:P + 96])):
                pool.dma_start(dst[:, :], src).then_inc(odd_in, 16)
            pool.wait_ge(odd_in, 48)
            for i in range(9):
                pool.wait_ge(qd32_done, i + 1)
                if i >= 2:
                    pool.wait_ge(qdr_done, i - 1)
                nc.gpsimd.tensor_tensor(qdc[:, i % 2, :], qd32[:, i % 2, :], cosD[:, :], ALU.mult).then_inc(qdc_done, 1)
            finish_pool(pool, 5)


        block = ctx.enter_context(nc.Block())

        @block.sync
        def _(sp):
            for u in range(2):
                sp.dma_start(raw[:, u, :], units[u * P:(u + 1) * P, :]).then_inc(raw_in[u], 16)

            def load(c, p):
                sp.wait_ge(w_lo, 2 * p + c - 1)
                sp.dma_start(raw[:, c % 2, :], units[bass.ds((c + 2 * p) * P, P), :]).then_inc(raw_in[c % 2], 16)

            with sp.Fori(0, (N_UNITS - 2) // 2) as p:
                load(2, p)
                load(3, p)
            if N_UNITS % 2:
                load(N_UNITS - 1, 0)
            for b in range(KD):
                sp.wait_ge(out_done, b + 1)
                sp.dma_start(out[b * P:(b + 1) * P, :], x[:, b, :]).then_inc(stored, 16)
            sp.wait_ge(stored, 16 * KD)

        @block.gpsimd
        def _(pool):
            nc.gpsimd.memset(ones[:, :], 1.0).then_inc(ones_set, 1)
            finish_pool(pool, 0)
            ffn_pool(pool, 0, 0)
            even_pool(pool)
            ffn_pool(pool, 1, 2)
            ffn_pool(pool, 2, 3)
            odd_pool(pool)
            ffn_pool(pool, 3, 5)

        @block.tensor
        def _(pe):
            pe.wait_ge(ones_set, 1)
            ffn_pe(pe, 0, U_FFN[0], 0)
            even_pe(pe)
            ffn_pe(pe, 1, U_FFN[1], 2)
            ffn_pe(pe, 2, U_FFN[2], 3)
            odd_pe(pe)
            ffn_pe(pe, 3, U_FFN[3], 5)
            norm_pe(pe, 6, 0)

        @block.scalar
        def _(act):
            act.dma_start(gain[:, :], gains).then_inc(const_in, 16)
            for b in range(KD):
                act.dma_start(x[:, b, :], xT[b * P:(b + 1) * P, :]).then_inc(x_in, 16)
            act.dma_start(cvec[:, :], colvec).then_inc(const_in, 16)
            act.dma_start(small[:, :], consts).then_inc(const_in, 16)
            act.dma_start(ident[:, :], ident_d).then_inc(const_in, 16)
            act.wait_ge(const_in, 64)
            act.wait_ge(x_in, 16 * KD)
            split_hi(act, 0)
            finish_act(act, 0)
            setup_act(act)
            ffn_act(act, 0, U_FFN[0], 0, False)
            even_act(act)
            ffn_act(act, 1, U_FFN[1], 2, False)
            ffn_act(act, 2, U_FFN[2], 3, False)
            odd_act(act)
            ffn_act(act, 3, U_FFN[3], 5, True)
            norm_act(act, 6, 0)

        @block.vector
        def _(dve):
            dve.wait_ge(const_in, 64)
            dve.wait_ge(x_in, 16 * KD)
            split_lo(dve, 0)
            for b in range(KD):
                lo_x(dve, 0, b)
            setup_dve(dve)
            ffn_dve(dve, 0, U_FFN[0], 0, False)
            even_dve(dve)
            ffn_dve(dve, 1, U_FFN[1], 2, False)
            ffn_dve(dve, 2, U_FFN[2], 3, False)
            odd_dve(dve)
            ffn_dve(dve, 3, U_FFN[3], 5, True)
            norm_dve(dve, 6)
            dve.wait_ge(rstd, 7)
            for b in range(KD):
                dve.wait_ge(sq_done, 8 * 7)
                nc.vector.scalar_tensor_tensor(x[:, b, :], x[:, b, :], gain[:, 6 * KD + b:6 * KD + b + 1],
                                               rB[:, :], ALU.mult, ALU.mult).then_inc(out_done, 1)


def unit_cols(w, width=256):
    k, n = w.shape
    return w.reshape(k // P, P, n // width, width).transpose(2, 1, 0, 3).reshape(-1, (k // P) * width)


def unit_rows(w):
    n, d = w.shape
    return w.reshape(n // 256, 2, P, d).transpose(0, 2, 1, 3).reshape(-1, 2 * d)


def padded(a):
    return np.concatenate([a, np.zeros((a.shape[0], UNIT - a.shape[1]), a.dtype)], axis=1)


def ffn_units(wg, wu, wd):
    g, u = (unit_cols(w).reshape(PAIRS, 1, P, UNIT) for w in (wg, wu))
    return [np.concatenate([g, u], axis=1).reshape(-1, UNIT), unit_rows(wd)]


def channels(v):
    return v.reshape(-1, P).T


def rope_rows(dim, rows, first):
    inv = (1.0 / (np.float32(10000.0) ** (np.arange(0, dim, 2, dtype=np.float32) / np.float32(dim)))).astype(np.float32)
    ang = (inv[:, None] * np.arange(SEQ, dtype=np.float32)[None, :]).astype(np.float32)
    reps = 2 * (rows - first) // dim
    c, s = (np.concatenate([f] + [g(ang).astype(np.float32)] * reps) for f, g in
            ((np.ones((first, SEQ), np.float32), np.cos), (np.zeros((first, SEQ), np.float32), np.sin)))
    return np.concatenate([c, s])


def rope_perm(dim, rows, first):
    m = np.zeros((rows, rows), np.float32)
    for r in range(first, rows):
        if (r - first) % dim < dim // 2:
            m[r + dim // 2, r] = -1.0
        else:
            m[r - dim // 2, r] = 1.0
    return m


def window_masks():
    m = np.full((3, 16, 8, WIN), NEG, np.float32)
    for k, t in ((0, 0), (1, 1), (2, 3)):
        for c in range(16):
            lo = min(max(16 * t + c - 8, 0), GRID_C - 16) - WSTART[t]
            m[k, c, :, lo:lo + 16] = 0.0
    return m.transpose(1, 2, 0, 3).reshape(P, 3 * WIN)


def kernel(**inputs):
    import concourse.bacc as bacc
    from concourse.bass_utils import run_bass_kernel_spmd

    i = {k: np.asarray(v) for k, v in inputs.items()}
    ev, od = i["ev_w_in"][0], i["od_w_in"][0]
    parts = []
    parts += ffn_units(i["ffn1_wg"][0], i["ffn1_wu"][0], i["ffn1_wd"][0])
    parts += [unit_cols(ev), unit_rows(i["ev_w_out"][0])]
    parts += ffn_units(i["ffn2_wg"][0], i["ffn2_wu"][0], i["ffn2_wd"][0])
    parts += ffn_units(i["ffn1_wg"][1], i["ffn1_wu"][1], i["ffn1_wd"][1])
    ckv_kr = np.concatenate([od[:, 1280:1408], od[:, 1344:1440], np.zeros((D, 32), od.dtype)], axis=1)
    gates = np.zeros((P, 2, 2, 4, P), od.dtype)
    for d in range(2):
        for k, w in enumerate((i["rg_wa"], i["rg_wx"])):
            for n in range(8):
                r = slice(64 * (n % 2), 64 * (n % 2) + 64)
                gates[r, d, k, n // 2, r] = w[0, d, n]
    uq = i["mla_wuq"][0].reshape(2, P, 768).transpose(1, 0, 2).reshape(P, 1536)
    parts += [unit_cols(od[:, 0:512]), unit_cols(od[:, 1024:1280]), unit_cols(ckv_kr), gates.reshape(P, UNIT),
              unit_cols(od[:, 512:1024]), padded(uq), padded(i["mla_wukv"][0]), unit_rows(i["od_w_out"][0])]
    parts += ffn_units(i["ffn2_wg"][1], i["ffn2_wu"][1], i["ffn2_wd"][1])
    units = np.concatenate(parts)
    assert units.shape == (N_UNITS * P, UNIT)

    norms = [i["ffn1_norm"][0], i["mix_norm"][0], i["ffn2_norm"][0], i["ffn1_norm"][1], i["mix_norm"][1],
             i["ffn2_norm"][1], i["final_norm"]]
    taps = np.concatenate([channels(i["conv_w"][0, j]) for j in range(4)], axis=1)
    colvec = np.concatenate([taps, channels(i["conv_b"][0]), channels(i["rg_ba"][0].reshape(-1)),
                             channels(i["rg_bx"][0].reshape(-1)), channels(i["rg_lam"][0].reshape(-1)),
                             channels(i["mla_gq"][0]), channels(i["mla_gkv"][0]), channels(i["diff_subln"][0])], axis=1)
    colvec = np.concatenate([colvec, np.zeros((P, 48 - colvec.shape[1]), colvec.dtype)], axis=1)
    small = np.zeros((P, 88), np.float32)
    small[:, 0] = EPS
    rpb = np.pad(i["na_rpb"][0][:, ::-1, ::-1], ((0, 0), (0, 0), (16, 17)))
    perm = np.zeros((P, P + 96), np.float32)
    perm[:, 0:P] = rope_perm(64, P, 0)
    perm[0:96, P:] = rope_perm(32, 96, 64)
    arrays = {
        "xT": i["x"][0].T, "units": units, "gains": np.concatenate([channels(g) for g in norms], axis=1),
        "consts": small, "colvec": colvec, "lamvec": i["diff_lam"][0].reshape(-1), "rpb": rpb.reshape(-1),
        "ident": np.eye(P, dtype=np.float32), "perm": perm, "rope_a": rope_rows(64, P, 0),
        "rope_d": rope_rows(32, 96, 64), "masks": window_masks(),
    }
    arrays = {k: np.ascontiguousarray(v) for k, v in arrays.items()}
    nc = bacc.Bacc("TRN2", target_bir_lowering=False, num_devices=1)
    args = [nc.dram_tensor("in_" + k, v.shape, mybir.dt.from_np(v.dtype), kind="ExternalInput").ap() for k, v in arrays.items()]
    args.append(nc.dram_tensor("outT", (D, SEQ), F32, kind="ExternalOutput").ap())
    build_trunk(nc, *args)
    r = run_bass_kernel_spmd(nc, [{"in_" + k: v for k, v in arrays.items()}], core_ids=[0])
    return np.ascontiguousarray(r.results[0]["outT"].T)[None]
```

```python
from contextlib import ExitStack

import numpy as np

import concourse.bass as bass
from concourse import mybir

ACT = mybir.ActivationFunctionType
ALU = mybir.AluOpType
AX = mybir.AxisListType.X
F32 = mybir.dt.float32
F32R = mybir.dt.float32r

P = 128
SEQ, D, FF = 512, 1024, 2816
KD = D // P
TT = SEQ // P
NF = FF // P
PAIRS = NF // 2
UNIT = 2048
EPS = 1e-6
GRID_R, GRID_C = 8, 64
WIN = 32
WSTART = (0, 8, 24, 32)
MTYPE = (0, 1, 1, 2)
NEG = -1.0e30

FFN_UNITS = 3 * PAIRS
EVEN_UNITS = 12 + 4
ODD_UNITS = 6 + 3 + 4
U_FFN = (0, FFN_UNITS + EVEN_UNITS, 2 * FFN_UNITS + EVEN_UNITS, 3 * FFN_UNITS + EVEN_UNITS + ODD_UNITS)
U_EVEN = FFN_UNITS
U_ODD = U_FFN[2] + FFN_UNITS
N_UNITS = 4 * FFN_UNITS + EVEN_UNITS + ODD_UNITS


def build_trunk(nc, xT, units, gains, consts, colvec, lamvec, rpb, ident_d, perm_d, rope_a, rope_d, masks_d, out):
    ctx = ExitStack()
    with ctx:
        def sem(name):
            return ctx.enter_context(nc.semaphore(name))

        def sb(name, shape, dt=F32, stack=ctx):
            return stack.enter_context(nc.sbuf_tensor(name, shape, dt))

        x = sb("x", [P, KD, SEQ])
        xgh = sb("xgh", [P, KD, SEQ], F32R)
        xgl = sb("xgl", [P, KD, SEQ], F32R)
        raw = sb("raw", [P, 2, UNIT])
        wh = sb("wh", [P, 2, UNIT], F32R)
        wl = sb("wl", [P, 2, UNIT], F32R)
        rB = sb("rB", [P, SEQ])
        sqt = sb("sqt", [P, 2, SEQ])
        std = sqt[:, 0, :]
        acc = sb("acc", [P, SEQ])
        ones = sb("ones", [P, P])
        ident = sb("ident", [P, P])
        gain = sb("gain", [P, 7 * KD])
        cvec = sb("cvec", [P, 48])
        small = sb("small", [P, 88])

        ffn_mem = ExitStack()
        ah = sb("ah", [P, NF, SEQ], F32R, ffn_mem)
        al = sb("al", [P, NF, SEQ], F32R, ffn_mem)
        tg = sb("tg", [P, 2, SEQ], F32, ffn_mem)
        sg = sb("sg", [P, 2, SEQ], F32, ffn_mem)
        ffn_mem.close()

        even_mem = ExitStack()
        oA = sb("oA", [P, 4, SEQ], F32, even_mem)
        relb = sb("relb", [P, 8, 8, 48], F32, even_mem)
        mask = acc[:, 0:3 * WIN].rearrange("p (m c) -> p m c", m=3)
        diff_mem = ExitStack()
        qah = sb("qah", [P, 4, SEQ], F32R, diff_mem)
        qal = sb("qal", [P, 4, SEQ], F32R, diff_mem)
        kah = sb("kah", [P, 4, SEQ], F32R, diff_mem)
        kal = sb("kal", [P, 4, SEQ], F32R, diff_mem)
        vah = sb("vah", [P, TT, 512], F32R, diff_mem)
        val = sb("val", [P, TT, 512], F32R, diff_mem)
        eA = sb("eA", [P, 2, 2, SEQ], F32, diff_mem)
        lamb = eA[:, 0, 0, 0:256]
        lamp = eA[:, 0, 1, 0:128].rearrange("p (a e) -> p a e", a=2)
        aT_mem = ExitStack()
        aTh = sb("aTh", [P, 2, TT, 2 * P], F32R, aT_mem)
        aTl = sb("aTl", [P, 2, TT, 2 * P], F32R, aT_mem)
        aT_mem.close()
        cosA = sb("cosA", [P, SEQ], F32, diff_mem)
        sinA = sb("sinA", [P, SEQ], F32, diff_mem)
        permA = sb("permA", [P, P], F32, diff_mem)
        q32 = sb("q32", [P, 2, SEQ], F32, diff_mem)
        qc = sb("qc", [P, 2, SEQ], F32, diff_mem)
        qs = sb("qs", [P, 2, SEQ], F32, diff_mem)
        diff_mem.close()
        qbh = sb("qbh", [P, 4, SEQ], F32R, even_mem)
        qbl = sb("qbl", [P, 4, SEQ], F32R, even_mem)
        kbh = sb("kbh", [P, 4, SEQ], F32R, even_mem)
        kbl = sb("kbl", [P, 4, SEQ], F32R, even_mem)
        vbh = sb("vbh", [P, TT, 512], F32R, even_mem)
        vbl = sb("vbl", [P, TT, 512], F32R, even_mem)
        pN = sb("pN", [P, 2, 5 * P], F32, even_mem)
        qb_mem = ExitStack()
        qb32 = sb("qb32", [P, 2, SEQ], F32, qb_mem)
        qb_mem.close()
        bTh = sb("bTh", [P, 2, 3, 2 * P], F32R, even_mem)
        bTl = sb("bTl", [P, 2, 3, 2 * P], F32R, even_mem)
        bm = sb("bm", [P, 2, 8, 8, WIN], F32, even_mem)
        sB = sqt[:, :, :].rearrange("p s (h k) -> p s h k", h=2)
        even_mem.close()

        odd_mem = ExitStack()
        cosD = sb("cosD", [96, SEQ], F32, odd_mem)
        sinD = sb("sinD", [96, SEQ], F32, odd_mem)
        permD = sb("permD", [96, 96], F32, odd_mem)
        cq_mem = ExitStack()
        cq = sb("cq", [P, 3, SEQ], F32, cq_mem)
        cqh = sb("cqh", [P, 3, SEQ], F32R, cq_mem)
        cql = sb("cql", [P, 3, SEQ], F32R, cq_mem)
        kpe = sb("kpe", [96, SEQ], F32, cq_mem)
        cq_mem.close()
        eD = sb("eD", [P, 2, 2, SEQ], F32, odd_mem)
        oD = sb("oD", [P, 4, SEQ], F32, odd_mem)
        dT_mem = ExitStack()
        dTh = sb("dTh", [P, 2, TT, 2 * P], F32R, dT_mem)
        dTl = sb("dTl", [P, 2, TT, 2 * P], F32R, dT_mem)
        dT_mem.close()
        rest = sb("rest", [P, 1024], F32, odd_mem)
        u_mem = ExitStack()
        uh = sb("uh", [P, 4, SEQ], F32R, u_mem)
        ul = sb("ul", [P, 4, SEQ], F32R, u_mem)
        u_mem.close()
        rg_mem = ExitStack()
        th = sb("th", [P, 8, SEQ], F32, rg_mem)
        xcp = sb("xcp", [P, 4, SEQ + 3], F32, rg_mem)
        gc = sb("gc", [P, 4, SEQ], F32, rg_mem)
        u32 = sb("u32", [P, 4, SEQ], F32, rg_mem)
        ra = sb("ra", [P, 8, SEQ], F32, rg_mem)
        iu = sb("iu", [P, 8, SEQ], F32, rg_mem)
        rg_mem.close()
        qd32 = sb("qd32", [96, 2, SEQ], F32, odd_mem)
        qdc = sb("qdc", [96, 2, SEQ], F32, odd_mem)
        qds = sb("qds", [96, 2, SEQ], F32, odd_mem)
        qdh = sb("qdh", [96, 8, SEQ], F32R, odd_mem)
        qdl = sb("qdl", [96, 8, SEQ], F32R, odd_mem)
        kdh = sb("kdh", [96, 8, SEQ], F32R, odd_mem)
        kdl = sb("kdl", [96, 8, SEQ], F32R, odd_mem)
        vdh, vdl = xgh[:, 4:8, :], xgl[:, 4:8, :]
        odd_mem.close()

        ps = ctx.enter_context(nc.psum_tensor("ps", [P, 8, 512], F32))

        C_EPS, C_NLAM = 0, 1
        C_RN = 4
        C_NMX, C_SUM, C_REC, C_CF = 12, 16, 20, 24
        C_LAM = 60
        C_M8, C_P8 = 64, 72
        C_TMP = 12
        recs = small[:, 80:88]
        V_CW, V_CB, V_BA, V_BX, V_LAM, V_GQ, V_GKV, V_SUB = 0, 16, 20, 28, 36, 44, 46, 47

        def col(c, n=1):
            return small[:, c:c + n]

        def vec(c, n=1):
            return cvec[:, c:c + n]

        x_in = [sem(f"x_in{b}") for b in range(KD)]
        gain_in = sem("gain_in")
        const_in = sem("const_in")
        ones_set = sem("ones_set")
        raw_in = [sem("raw_in0"), sem("raw_in1")]
        w_hi = sem("w_hi")
        w_lo = sem("w_lo")
        w_hi_part = sem("w_hi_part")
        w_lo_part = sem("w_lo_part")
        w_half = sem("w_half")
        x_new = sem("x_new")
        xg_hi = sem("xg_hi")
        xg_lo = sem("xg_lo")
        sq_done = sem("sq_done")
        sq_sum = sem("sq_sum")
        ssum_done = sem("ssum_done")
        std_done = sem("std_done")
        rstd = sem("rstd")
        tg_done = sem("tg_done")
        silu_done = sem("silu_done")
        s2_done = sem("s2_done")
        a32_done = sem("a32_done")
        a_hi = sem("a_hi")
        a_lo = sem("a_lo")
        y_done = sem("y_done")
        out_done = sem("out_done")
        stored = sem("stored")
        setup = sem("setup")

        even_in = sem("even_in")


        def split_hi(act, c, p=0, n=UNIT):
            act.wait_ge(raw_in[c % 2], 16 * p + 16 * (c // 2 + 1))
            if c >= 2:
                act.wait_ge(w_half, 4 * p + 2 * (c - 1))
            nc.scalar.activation(wh[:, c % 2, 0:n], raw[:, c % 2, 0:n], ACT.Copy).then_inc(w_hi, 1)

        def split_lo(dve, c, p=0, n=UNIT):
            dve.wait_ge(w_hi, 2 * p + c + 1)
            nc.vector.tensor_tensor(wl[:, c % 2, 0:n], raw[:, c % 2, 0:n], wh[:, c % 2, 0:n].bitcast(F32),
                                    ALU.subtract).then_inc(w_lo, 1)

        def quarter(q):
            return slice(q * UNIT // 4, (q + 1) * UNIT // 4)

        def split_hi_part(act, c, q, nth):
            if q == 0:
                act.wait_ge(raw_in[c % 2], 16 * (c // 2 + 1))
                act.wait_ge(w_half, 2 * (c - 1))
            ins = nc.scalar.activation(wh[:, c % 2, quarter(q)], raw[:, c % 2, quarter(q)], ACT.Copy)
            ins.then_inc(w_hi if q == 3 else w_hi_part, 1)

        def split_lo_part(pool, c, q, nth):
            if q < 3:
                pool.wait_ge(w_hi_part, 3 * nth + q + 1)
            else:
                pool.wait_ge(w_hi, c + 1)
                pool.wait_ge(w_lo, c)
            ins = nc.gpsimd.tensor_tensor(wl[:, c % 2, quarter(q)], raw[:, c % 2, quarter(q)],
                                          wh[:, c % 2, quarter(q)].bitcast(F32), ALU.subtract)
            if q == 3:
                ins.then_inc(w_lo, 1)
            else:
                ins.then_inc(w_lo_part, 1)

        def three(dst, lh, ll, rh, rl, first, last):
            nc.tensor.matmul(dst, lh, rh, start=first, stop=False)
            nc.tensor.matmul(dst, lh, rl, start=False, stop=False)
            return nc.tensor.matmul(dst, ll, rh, start=False, stop=last)

        def block_T(pe, dst, c, m, width=P, step=256, nt=KD, wait_x=None):
            s = c % 2
            for k in range(nt):
                if wait_x is not None:
                    pe.wait_ge(xg_lo, wait_x + k + 1)
                o = k * step + m * P
                mm = three(dst, wh[:, s, o:o + width], wl[:, s, o:o + width],
                           xgh[:, k, :], xgl[:, k, :], k == 0, k == nt - 1)
            return mm

        def finish_dve(dve, n, scale, last_unit, held=KD, split=None):
            for b in range(KD):
                if b == KD // 2 and split is not None:
                    split_lo(dve, split)
                if b < KD - 1:
                    dve.wait_ge(y_done, 7 * (n - 1) + b + 1)
                else:
                    dve.wait_ge(w_half, 2 * (last_unit + 1))
                nc.vector.scalar_tensor_tensor(x[:, b, :], ps[:, b, :], scale, x[:, b, :],
                                               ALU.mult, ALU.add).then_inc(x_new, 1)
                if b >= 1 and n < 6 and b <= held:
                    lo_x(dve, n, b - 1)
            for b in range(held, KD) if held < KD else (KD - 1,):
                if n < 6:
                    lo_x(dve, n, b)

        def lo_x(dve, n, b):
            dve.wait_ge(xg_hi, 8 * n + b + 1)
            nc.vector.scalar_tensor_tensor(xgl[:, b, :], x[:, b, :], gain[:, n * KD + b:n * KD + b + 1],
                                           xgh[:, b, :].bitcast(F32), ALU.mult, ALU.subtract).then_inc(xg_lo, 1)

        def finish_act(act, n, last_unit=None, held=KD, split=None):
            for b in range(KD):
                if b == KD // 2 and split is not None:
                    split_hi(act, split)
                if n:
                    act.wait_ge(x_new, 8 * (n - 1) + b + 1)
                else:
                    act.wait_ge(x_in[b], 16)
                if n < 6 and b < held:
                    if b >= 6 and last_unit is not None:
                        act.wait_ge(w_half, 2 * (last_unit + 1))
                    nc.scalar.activation(xgh[:, b, :], x[:, b, :], ACT.Copy,
                                         scale=gain[:, n * KD + b:n * KD + b + 1]).then_inc(xg_hi, 1)
                if b == 0 and n:
                    act.wait_ge(ssum_done, n)
                if b == 1 and n:
                    act.wait_ge(sq_sum, 7 * n)
                if b >= 3:
                    act.wait_ge(sq_sum, 7 * n + b - 2)
                dst = acc[:, :] if b == 0 else sqt[:, b % 2, :]
                nc.scalar.activation(dst, x[:, b, :], ACT.Square).then_inc(sq_done, 1)
            for b in range(held, KD):
                act.wait_ge(w_half, 2 * (last_unit + 1))
                nc.scalar.activation(xgh[:, b, :], x[:, b, :], ACT.Copy,
                                     scale=gain[:, n * KD + b:n * KD + b + 1]).then_inc(xg_hi, 1)

        def finish_pool(pool, n):
            for b in range(1, KD):
                pool.wait_ge(sq_done, 8 * n + b + 1)
                if b >= 2:
                    pool.wait_ge(sq_sum, 7 * n + b - 1)
                nc.gpsimd.tensor_tensor(acc[:, :], acc[:, :], sqt[:, b % 2, :], ALU.add).then_inc(sq_sum, 1)

        def norm_pe(pe, n, bank):
            pe.wait_ge(sq_sum, 7 * (n + 1))
            nc.tensor.matmul(ps[:, bank, :], ones[:, :], acc[:, :], start=True, stop=True).then_inc(ssum_done, 1)

        def norm_act(act, n, bank):
            act.wait_ge(ssum_done, n + 1)
            if n:
                act.wait_ge(rstd, n)
            nc.scalar.activation(std, ps[:, bank, :], ACT.Sqrt, bias=col(C_EPS),
                                 scale=1.0 / D).then_inc(std_done, 1)

        def norm_dve(dve, n):
            dve.wait_ge(std_done, n + 1)
            nc.vector.reciprocal(rB[:, :], std).then_inc(rstd, 1)


        def ffn_up_pe(pe, f, B, n, p):
            first = isinstance(p, int)
            c0, c1 = B, B + 1
            pe.wait_ge(w_lo, 2 * p + c0 + 1)
            if not first:
                pe.wait_ge(tg_done, 2 * p + 22 * f)
            for m in range(2):
                block_T(pe, ps[:, m, :], c0, m, wait_x=8 * n if first and m == 0 else None).then_inc(w_half, 1)
                if first and m == 0:
                    norm_pe(pe, n, 4)
            pe.wait_ge(w_lo, 2 * p + c1 + 1)
            if not first:
                pe.wait_ge(a32_done, 2 * p + 22 * f)
            for m in range(2):
                block_T(pe, ps[:, 2 + m, :], c1, m).then_inc(w_half, 1)

        def down_pe(pe, c, p, kt, src_h, src_l, first):
            s = c % 2
            pe.wait_ge(w_lo, 2 * p + c + 1)
            for k2 in range(2):
                for b in (4, 5, 6, 7, 0, 1, 2, 3):
                    o = k2 * D + b * P
                    mm = three(ps[:, b, :], wh[:, s, o:o + P], wl[:, s, o:o + P],
                               src_h[:, bass.ds(kt + k2, 1), :], src_l[:, bass.ds(kt + k2, 1), :],
                               first and k2 == 0, False)
                mm.then_inc(w_half, 1)

        def down_last_pe(pe, c, kt, src_h, src_l):
            s = c % 2
            pe.wait_ge(w_lo, c + 1)
            for b in range(KD):
                for k2 in range(2):
                    o = k2 * D + b * P
                    mm = three(ps[:, b, :], wh[:, s, o:o + P], wl[:, s, o:o + P],
                               src_h[:, kt + k2, :], src_l[:, kt + k2, :], False, k2 == 1)
                if b < KD - 1:
                    mm.then_inc(y_done, 1)
                else:
                    mm.then_inc(w_half, 2)

        def ffn_pe(pe, f, B, n):
            ffn_up_pe(pe, f, B, n, 0)
            with pe.Fori(1, PAIRS) as p:
                ffn_up_pe(pe, f, B, n, p)
            c = B + 2 * PAIRS
            pe.wait_ge(a_lo, 22 * f + NF - 2)
            pe.wait_ge(std_done, n + 1)
            s = c % 2
            pe.wait_ge(w_lo, c + 1)
            for k2 in range(2):
                for b in (4, 5, 6, 7, 0, 1, 2, 3):
                    if k2 == 0 and b == 0:
                        pe.wait_ge(a32_done, 22 * (f + 1))
                    o = k2 * D + b * P
                    mm = three(ps[:, b, :], wh[:, s, o:o + P], wl[:, s, o:o + P],
                               ah[:, k2, :], al[:, k2, :], k2 == 0, False)
                mm.then_inc(w_half, 1)
            pe.wait_ge(a_lo, 22 * (f + 1))
            with pe.Fori(0, (PAIRS - 3) // 2) as j:
                for t in range(2):
                    down_pe(pe, c + 1 + t, j, 4 * j + 2 + 2 * t, ah, al, False)
            down_pe(pe, c + 9, 0, 18, ah, al, False)
            down_last_pe(pe, c + 10, 20, ah, al)

        def ffn_act(act, f, B, n, last):
            def pair(p, at_start):
                split_hi(act, B + 1, p)
                if at_start:
                    norm_act(act, n, 4)
                for m in range(2):
                    act.wait_ge(tg_done, 2 * p + 22 * f + m + 1)
                    nc.scalar.activation(sg[:, m, :], tg[:, m, :], ACT.Silu).then_inc(silu_done, 1)
                split_hi(act, B + 2, p)
                for m in range(2):
                    act.wait_ge(a32_done, 2 * p + 22 * f + m + 1)
                    nc.scalar.activation(ah[:, bass.ds(2 * p + m, 1), :], tg[:, m, :], ACT.Copy).then_inc(a_hi, 1)

            pair(0, True)
            with act.Fori(1, PAIRS) as p:
                pair(p, False)
            c = B + 2 * PAIRS
            with act.Fori(0, (PAIRS - 1) // 2) as j:
                split_hi(act, c + 1, j)
                split_hi(act, c + 2, j)
            if not last:
                split_hi(act, c + PAIRS)
            finish_act(act, n + 1)

        def ffn_dve(dve, f, B, n, last):
            def pair(p, at_start):
                split_lo(dve, B + 1, p)
                if at_start:
                    norm_dve(dve, n)
                    dve.wait_ge(rstd, n + 1)
                if f or not at_start:
                    dve.wait_ge(a_lo, 2 * p + 22 * f)
                for m in range(2):
                    dve.wait_ge(w_half, 4 * p + 2 * B + m + 1)
                    nc.vector.tensor_tensor(tg[:, m, :], ps[:, m, :], rB[:, :], ALU.mult).then_inc(tg_done, 1)
                split_lo(dve, B + 2, p)
                for m in range(2):
                    dve.wait_ge(w_half, 4 * p + 2 * B + m + 3)
                    dve.wait_ge(s2_done, 2 * p + 22 * f + m + 1)
                    nc.vector.tensor_tensor(tg[:, m, :], ps[:, 2 + m, :], sg[:, m, :], ALU.mult).then_inc(a32_done, 1)
                for m in range(2):
                    dve.wait_ge(a_hi, 2 * p + 22 * f + m + 1)
                    nc.vector.tensor_tensor(al[:, bass.ds(2 * p + m, 1), :], tg[:, m, :],
                                            ah[:, bass.ds(2 * p + m, 1), :].bitcast(F32),
                                            ALU.subtract).then_inc(a_lo, 1)

            pair(0, True)
            with dve.Fori(1, PAIRS) as p:
                pair(p, False)
            c = B + 2 * PAIRS
            with dve.Fori(0, (PAIRS - 1) // 2) as j:
                split_lo(dve, c + 1, j)
                split_lo(dve, c + 2, j)
            if not last:
                split_lo(dve, c + PAIRS)
            finish_dve(dve, n + 1, 0.5, c + PAIRS - 1)

        def ffn_pool(pool, f, n):
            pool.wait_ge(rstd, n + 1)
            with pool.Fori(0, PAIRS) as p:
                for m in range(2):
                    pool.wait_ge(silu_done, 2 * p + 22 * f + m + 1)
                    nc.gpsimd.tensor_tensor(sg[:, m, :], sg[:, m, :], rB[:, :], ALU.mult).then_inc(s2_done, 1)
            finish_pool(pool, n + 1)

        q32_done = sem("q32_done")
        qc_done = sem("qc_done")
        rot_done = sem("rot_done")
        qs_done = sem("qs_done")
        qr_done = sem("qr_done")
        qa_hi = sem("qa_hi")
        qa_lo = sem("qa_lo")
        va_hi = sem("va_hi")
        va_lo = sem("va_lo")
        rcol_done = sem("rcol_done")
        rcol_read = sem("rcol_read")
        lam_done = sem("lam_done")
        lam_exp = sem("lam_exp")
        sa_done = sem("sa_done")
        mxa_done = sem("mxa_done")
        ea_done = sem("ea_done")
        reca_done = sem("reca_done")
        map2_done = sem("map2_done")
        wa_done = sem("wa_done")
        ta_done = sem("ta_done")
        ah_done = sem("ah_done")
        al_done = sem("al_done")
        pa_done = sem("pa_done")
        oa_done = sem("oa_done")
        ssa_done = sem("ssa_done")
        asum_done = sem("asum_done")
        arms_done = sem("arms_done")
        rsa_done = sem("rsa_done")
        oan_done = sem("oan_done")
        mix_hi = sem("mix_hi")
        mix_lo = sem("mix_lo")
        mask_in = sem("mask_in")
        qb32_done = sem("qb32_done")
        qb_hi = sem("qb_hi")
        qb_lo = sem("qb_lo")
        vt_done = sem("vt_done")
        vb_hi = sem("vb_hi")
        vb_lo = sem("vb_lo")
        bm_done = sem("bm_done")
        pn_zero = sem("pn_zero")
        wo_done = sem("wo_done")
        wo_read = sem("wo_read")
        odd_in = sem("odd_in")
        in_read = sem("in_read")
        pad_done = sem("pad_done")
        u_done = sem("u_done")
        u_hi = sem("u_hi")
        u_lo = sem("u_lo")
        gate_done = sem("gate_done")
        sig_done = sem("sig_done")
        th_done = sem("th_done")
        tmax_done = sem("tmax_done")
        a_done = sem("a_done")
        asq_done = sem("asq_done")
        asqo_done = sem("asqo_done")
        vv_done = sem("vv_done")
        mult_done = sem("mult_done")
        one_done = sem("one_done")
        iu_done = sem("iu_done")
        bt_done = sem("bt_done")
        h_done = sem("h_done")
        hs_done = sem("hs_done")
        gelu_done = sem("gelu_done")
        oc_done = sem("oc_done")
        omix_hi = sem("omix_hi")
        omix_lo = sem("omix_lo")
        csq_done = sem("csq_done")
        csq_sum = sem("csq_sum")
        cs_done = sem("cs_done")
        cstd_done = sem("cstd_done")
        crs_done = sem("crs_done")
        cqn_done = sem("cqn_done")
        cq_hi = sem("cq_hi")
        cq_lo = sem("cq_lo")
        qd_ps = sem("qd_ps")
        kd_ps = sem("kd_ps")
        vd_ps = sem("vd_ps")
        qd32_done = sem("qd32_done")
        qdc_done = sem("qdc_done")
        rotd_done = sem("rotd_done")
        qds_done = sem("qds_done")
        qdr_done = sem("qdr_done")
        qd_hi = sem("qd_hi")
        qd_lo = sem("qd_lo")
        kd_hi = sem("kd_hi")
        kd_lo = sem("kd_lo")
        kr_hi = sem("kr_hi")
        kr_lo = sem("kr_lo")
        vd_hi = sem("vd_hi")
        vd_lo = sem("vd_lo")
        mxraw = sem("mxraw")
        setup_act_done = sem("setup_act_done")
        STEP_SEMS = ("scores", "max", "exp", "rec", "turned", "hi", "lo", "pv")
        SN = {n: sem("n_" + n) for n in STEP_SEMS + ("scores_read", "o_hi", "o_lo")}
        SM = {n: sem("m_" + n) for n in STEP_SEMS + ("o",)}
        n_norm = sem("n_norm")
        n_norm2 = sem("n_norm2")
        m_norm = sem("m_norm")
        m_norm2 = sem("m_norm2")

        TMP = [small[:, C_TMP + 8 * i:C_TMP + 8 * i + 8] for i in range(6)]
        NLAM, EXPL, SS1, SS2, POLY, SPT = TMP

        def setup_act(act):
            act.wait_ge(setup, 2)
            nc.scalar.activation(EXPL, EXPL, ACT.Exp, scale=-1.0).then_inc(setup_act_done, 1)

        def setup_dve(dve):
            n = [0]

            def step(ins):
                n[0] += 1
                ins.then_inc(setup, 1)
                dve.wait_ge(setup, n[0])

            lam = vec(V_LAM, 8)
            step(nc.vector.tensor_scalar(NLAM, lam, -1.0, None, ALU.mult))
            step(nc.vector.tensor_tensor(EXPL, NLAM, lam, ALU.max))
            dve.wait_ge(setup_act_done, 1)
            step(nc.vector.tensor_scalar(SS2, EXPL, 2.0, None, ALU.add))
            step(nc.vector.reciprocal(SS1, SS2))
            step(nc.vector.tensor_tensor(SS1, SS1, EXPL, ALU.mult))
            step(nc.vector.tensor_tensor(SS2, SS1, SS1, ALU.mult))
            step(nc.vector.tensor_scalar(POLY, SS2, 1.0 / 13, 1.0 / 11, ALU.mult, ALU.add))
            for k in (9, 7, 5, 3, 1):
                step(nc.vector.tensor_tensor(POLY, POLY, SS2, ALU.mult))
                step(nc.vector.tensor_scalar(POLY, POLY, 1.0 / k, None, ALU.add))
            step(nc.vector.tensor_tensor(POLY, POLY, SS1, ALU.mult))
            step(nc.vector.tensor_scalar(SPT, NLAM, 0.0, None, ALU.max))
            step(nc.vector.scalar_tensor_tensor(SPT, POLY, 2.0, SPT, ALU.mult, ALU.add))
            step(nc.vector.tensor_scalar(col(C_M8, 8), SPT, -8.0, None, ALU.mult))
            step(nc.vector.tensor_scalar(col(C_P8, 8), SPT, 8.0, None, ALU.mult))

        def norm_reads_pe(pe):
            pe.wait_ge(rstd, 2)
            for t in range(TT):
                mm = nc.tensor.matmul(ps[:, 5, t:t + 1], rB[0:1, t * P:(t + 1) * P], ones[0:1, 0:1],
                                      start=True, stop=True)
            mm.then_inc(rcol_done, 1)

        def block_V(dst, c, k_ap, width, step):
            s = c % 2
            for k in range(KD):
                mm = three(dst, k_ap(xgh, k), k_ap(xgl, k), wh[:, s, k * step:k * step + width],
                           wl[:, s, k * step:k * step + width], k == 0, k == KD - 1)
            return mm

        BE = U_EVEN
        LAM_INIT = 0.8 - 0.6 * 1.0
        QS = 64 ** -0.5

        def rot_pe(pe, i):
            pe.wait_ge(q32_done, i + 1)
            if i >= 2:
                pe.wait_ge(qs_done, i - 1)
            nc.tensor.matmul(ps[:, 2 + i % 2, :], permA[:, :], q32[:, i % 2, :],
                             start=True, stop=True).then_inc(rot_done, 1)

        def aT_of(buf, j):
            return buf[:, j // 2 % 2, :, (j % 2) * P:(j % 2 + 1) * P]

        def bank_of(j):
            return ps[:, 4 + j % 2, :].rearrange("p (k q) -> p k q", k=TT)

        def diff_scores_pe(pe, i):
            a, t, b = i // 4, i % 4, 2 * (i % 2)
            if i >= 2:
                pe.wait_ge(ea_done, 2 * (i - 1))
            for m in range(2):
                r = slice(64 * m, 64 * m + 64)
                three(ps[:, b + m, :], qah[r, a, t * P:(t + 1) * P], qal[r, a, t * P:(t + 1) * P],
                      kah[r, a, :], kal[r, a, :], True, True).then_inc(sa_done, 1)

        def diff_max_dve(dve, i):
            b = 2 * (i % 2)
            dve.wait_ge(sa_done, 2 * i + 2)
            nc.vector.tensor_reduce(col(C_NMX + b, 2), ps[:, b:b + 2, :], AX, ALU.max,
                                    negate=True).then_inc(mxa_done, 1)

        def diff_exp_act(act, i):
            act.wait_ge(mxa_done, i + 1)
            if i >= 2:
                act.wait_ge(ta_done, i - 1)
            for m in range(2):
                nc.scalar.activation(eA[:, i % 2, m, :], ps[:, 2 * (i % 2) + m, :], ACT.Exp,
                                     bias=col(C_NMX + 2 * (i % 2) + m),
                                     accum_out=col(C_SUM + 2 * (i % 2) + m)).then_inc(ea_done, 1)

        def na_block_pe(pe, i):
            c = BE + 6 + i // 2
            pe.wait_ge(w_lo, c + 1)
            if i >= 2:
                pe.wait_ge(qb32_done, i - 1)
            else:
                pe.wait_ge(ea_done, 32)
            block_T(pe, ps[:, i % 2, :], c, i % 2).then_inc(w_half, 1)

        def diff_pe(pe):
            for i in range(19):
                if 2 <= i < 16:
                    diff_scores_pe(pe, i)
                j = i - 2
                if 0 <= j < 16:
                    if j == 0:
                        pe.wait_ge(va_lo, 8)
                    pe.wait_ge(wa_done, j + 1)
                    if j >= 2:
                        pe.wait_ge(al_done, j - 1)
                    for k in range(TT):
                        mm = nc.tensor.transpose(ps[:, 4 + j % 2, k * P:(k + 1) * P],
                                                 eA[:, j % 2, 0, k * P:(k + 1) * P], ident[:, :])
                    mm.then_inc(ta_done, 1)
                u = (i - 3) // 2
                if i % 2 == 0 and 0 <= u < 8:
                    a = u // 2
                    pe.wait_ge(al_done, 2 * u + 2)
                    if u >= 2:
                        pe.wait_ge(oa_done, u - 1)
                    for k in range(TT):
                        mm = three(ps[:, 6 + u % 2, 0:2 * P], vah[:, k, a * P:(a + 1) * P],
                                   val[:, k, a * P:(a + 1) * P], aTh[:, u % 2, k, :], aTl[:, u % 2, k, :],
                                   k == 0, k == TT - 1)
                    mm.then_inc(pa_done, 1)
                if i == 17:
                    na_block_pe(pe, 0)

        def diff_act(act):
            for i in range(21):
                j = i - 2
                if 0 <= j < 16:
                    act.wait_ge(ta_done, j + 1)
                    if j >= 4:
                        act.wait_ge(pa_done, j // 2 - 1)
                    nc.scalar.activation(aT_of(aTh, j), bank_of(j), ACT.Copy).then_inc(ah_done, 1)
                u = (i - 4) // 2
                if i % 2 and 0 <= u < 8:
                    act.wait_ge(pa_done, u + 1)
                    nc.scalar.activation(oA[:, u // 2, 2 * P * (u % 2):2 * P * (u % 2 + 1)],
                                         ps[:, 6 + u % 2, 0:2 * P], ACT.Copy).then_inc(oa_done, 1)
                if 2 <= i < 16:
                    diff_exp_act(act, i)
                if i == 18:
                    split_hi(act, BE + 7)

        def diff_pool(pool):
            for j in range(16):
                pool.wait_ge(reca_done, 2 * j + 2)
                nc.gpsimd.tensor_tensor(eA[:, j % 2, 1, :], eA[:, j % 2, 1, :],
                                        col(C_CF + 2 * (j % 2)).broadcast_to([P, SEQ]), ALU.mult).then_inc(map2_done, 1)

        def diff_rec_dve(dve, j):
            b = 2 * (j % 2)
            dve.wait_ge(ea_done, 2 * j + 2)
            nc.vector.reciprocal(col(C_REC + b, 2), col(C_SUM + b, 2)).then_inc(reca_done, 1)
            dve.wait_ge(reca_done, 2 * j + 1)
            nc.vector.tensor_tensor(col(C_CF + b), col(C_REC + b + 1), col(C_NLAM),
                                    ALU.mult).then_inc(reca_done, 1)

        def diff_comb_dve(dve, j):
            b = 2 * (j % 2)
            dve.wait_ge(map2_done, j + 1)
            nc.vector.scalar_tensor_tensor(eA[:, j % 2, 0, :], eA[:, j % 2, 0, :], col(C_REC + b),
                                           eA[:, j % 2, 1, :], ALU.mult, ALU.add).then_inc(wa_done, 1)

        def diff_dve(dve):
            for i in range(20):
                j = i - 1
                if 1 <= j < 16:
                    diff_rec_dve(dve, j)
                if 2 <= i < 16:
                    diff_max_dve(dve, i)
                j = i - 2
                if 0 <= j < 16:
                    dve.wait_ge(ah_done, j + 1)
                    nc.vector.tensor_tensor(aT_of(aTl, j), bank_of(j), aT_of(aTh, j).bitcast(F32),
                                            ALU.subtract).then_inc(al_done, 1)
                j = i - 1
                if 1 <= j < 16:
                    diff_comb_dve(dve, j)
                if i == 18:
                    split_lo(dve, BE + 7)

        def diff_norm_pe(pe, a):
            pe.wait_ge(ssa_done, a + 1)
            nc.tensor.matmul(ps[:, 4 + a, :], ones[:, :], sqt[:, a % 2, :], start=True, stop=True).then_inc(asum_done, 1)

        def diff_norm_act(act, a0):
            for a in (a0, a0 + 1):
                act.wait_ge(oa_done, 2 * a + 2)
                if a >= 2:
                    act.wait_ge(oan_done, a - 1)
                nc.scalar.activation(sqt[:, a % 2, :], oA[:, a, :], ACT.Square).then_inc(ssa_done, 1)

        def diff_sqrt_act(act, a0):
            for a in (a0, a0 + 1):
                act.wait_ge(asum_done, a + 1)
                nc.scalar.activation(sqt[:, a % 2, :], ps[:, 4 + a, :], ACT.Sqrt, bias=col(C_EPS),
                                     scale=1.0 / P).then_inc(arms_done, 1)

        def diff_norm_dve(dve, a):
            dve.wait_ge(arms_done, a + 1)
            nc.vector.reciprocal(sqt[:, a % 2, :], sqt[:, a % 2, :]).then_inc(rsa_done, 1)
            dve.wait_ge(rsa_done, a + 1)
            nc.vector.scalar_tensor_tensor(oA[:, a, :], oA[:, a, :], vec(V_SUB), sqt[:, a % 2, :],
                                           ALU.mult, ALU.mult).then_inc(oan_done, 1)

        def na_step(i):
            tp, h = i // 8, i % 8
            return tp, h, h // 2, slice(64 * (h % 2), 64 * (h % 2) + 64)

        def na_tile(i, t):
            tp = i // 8
            inner = t != tp
            return inner, (slice(0, 3) if inner else slice(0, 2) if tp == 0 else slice(1, 3))

        def na_probs(i, t):
            return pN[:, i % 2, 0:3 * P] if na_tile(i, t)[0] else pN[:, i % 2, 3 * P:5 * P]

        def na_window(i, t):
            return pN[:, i % 2, 64:64 + 8 * WIN] if na_tile(i, t)[0] else pN[:, i % 2, 3 * P:5 * P]

        NA_SPLITS = {3 + q: (BE + 13, q, 0) for q in range(4)} | {11 + q: (BE + 14, q, 1) for q in range(4)}

        def na_scores_pe(pe, i):
            tp, h, hp, rows = na_step(i)
            if i >= 2:
                pe.wait_ge(SN["scores_read"], i - 1)
            for t in range(2):
                w, q0 = WSTART[2 * tp + t], (2 * tp + t) * P
                keys = [k[rows, hp, :].rearrange("p (r c) -> p r c", r=GRID_R)[:, :, w:w + WIN]
                        for k in (kbh, kbl)]
                q = [k[rows, hp, q0:q0 + P] for k in (qbh, qbl)]
                three(ps[:, 4 + i % 2, t * 8 * WIN:(t + 1) * 8 * WIN], *q, *keys, True, True).then_inc(SN["scores"], 1)

        def na_pe(pe):
            for i in range(19):
                j = i - 2
                if 0 <= j < 16:
                    if j == 0:
                        pe.wait_ge(qb32_done, 12)
                        pe.wait_ge(vb_lo, 4)
                    for t in range(2):
                        z = 2 * j + t
                        inner, kk = na_tile(j, t)
                        pe.wait_ge(n_norm2 if inner else n_norm, j + 1)
                        if z >= 3:
                            pe.wait_ge(SN["lo"], z - 2)
                        for k in range(kk.stop - kk.start):
                            mm = nc.tensor.transpose(ps[:, z % 3, k * P:(k + 1) * P],
                                                     na_probs(j, t)[:, k * P:(k + 1) * P], ident[:, :])
                        mm.then_inc(SN["turned"], 1)
                if 2 <= i < 16:
                    na_scores_pe(pe, i)
                if 3 <= i:
                    wo_first_pe(pe, 2 * (i - 3))
                j = i - 3
                if 0 <= j < 16:
                    tp, _, hp, _ = na_step(j)
                    pe.wait_ge(SN["lo"], 2 * j + 2)
                    if j >= 2:
                        pe.wait_ge(SN["o_lo"], j - 1)
                    outer = slice(0, P) if tp == 0 else slice(P, 2 * P)
                    inner = slice(P, 2 * P) if tp == 0 else slice(0, P)
                    parts = [(tp, slice(0, 2 * P)), (tp + 1, slice(0, 2 * P)), (2 - 2 * tp, inner)]
                    for n, (kk, cs) in enumerate(parts):
                        v = [k[:, tp + kk, hp * P:(hp + 1) * P] for k in (vbh, vbl)]
                        mm = three(ps[:, 3 + 3 * (j % 2), cs], *v, bTh[:, j % 2, kk, cs], bTl[:, j % 2, kk, cs], n == 0, n == 2)
                    mm.then_inc(SN["pv"], 1)
                if 3 <= i:
                    wo_first_pe(pe, 2 * (i - 3) + 1)

        def grid_cols(ap, tp):
            return ap.rearrange("p (r c) -> p c r", r=GRID_R)[:, 32 * tp:32 * tp + 32, :]

        def wo_first_pe(pe, z):
            b, k = z // 4, z % 4
            c = BE + 12 + b // 4
            s = c % 2
            if k == 0:
                pe.wait_ge(w_lo, c + 1)
                if b:
                    pe.wait_ge(wo_read, b)
            if b == 0:
                pe.wait_ge(mix_lo, k + 1)
            o = k * 512 + (b % 4) * P
            mm = three(ps[:, 7, :], wh[:, s, o:o + P], wl[:, s, o:o + P], xgh[:, k, :], xgl[:, k, :], k == 0, k == 3)
            if k == 3:
                mm.then_inc(*((w_half, 2) if b % 4 == 3 else (wo_done, 1)))

        def wo_first_dve(dve, b):
            if b % 4 == 3:
                dve.wait_ge(w_half, 2 * (BE + 12 + b // 4 + 1))
            else:
                dve.wait_ge(wo_done, b - b // 4 + 1)
            nc.vector.tensor_tensor(x[:, b, :], ps[:, 7, :], x[:, b, :], ALU.add).then_inc(wo_read, 1)

        def wo_second_pe(pe):
            for b in range(KD):
                c = BE + 14 + b // 4
                s = c % 2
                pe.wait_ge(w_lo, c + 1)
                if b == 0:
                    pe.wait_ge(SN["lo"], 32)
                if b == 7:
                    pe.wait_ge(wo_read, 8)
                for k in range(4):
                    if b == 0:
                        pe.wait_ge(SN["o_lo"], (10, 12, 14, 16)[k])
                    o = k * 512 + (b % 4) * P
                    mm = three(ps[:, b, :], wh[:, s, o:o + P], wl[:, s, o:o + P],
                               xgh[:, 4 + k, :], xgl[:, 4 + k, :], k == 0, k == 3)
                    if b == 4 and k == 0:
                        mm.then_inc(y_done, 1)
                mm.then_inc(*((w_half, 2) if b % 4 == 3 else (y_done, 1)))

        def na_exp_act(act, i):
            act.wait_ge(SN["max"], i + 1)
            if i >= 2:
                act.wait_ge(SN["turned"], 2 * (i - 1))
            if i == 0:
                act.wait_ge(pn_zero, 1)
            for t in range(2):
                c = 2 * (i % 2) + t
                nc.scalar.activation(na_window(i, t).rearrange("p (c j) -> p j c", j=8),
                                     sB[:, i % 2, t, :].rearrange("p (j c) -> p j c", j=8),
                                     ACT.Exp, bias=col(C_NMX + c),
                                     accum_out=col(C_SUM + c)).then_inc(SN["exp"], 1)

        def na_act(act):
            for i in range(20):
                j = i - 2
                if 0 <= j < 16:
                    if j >= 2:
                        act.wait_ge(SN["pv"], j - 1)
                    for t in range(2):
                        z = 2 * j + t
                        kk = na_tile(j, t)[1]
                        n = kk.stop - kk.start
                        act.wait_ge(SN["turned"], z + 1)
                        nc.scalar.activation(bTh[:, j % 2, kk, t * P:(t + 1) * P],
                                             ps[:, z % 3, 0:n * P].rearrange("p (k q) -> p k q", k=n),
                                             ACT.Copy).then_inc(SN["hi"], 1)
                j = i - 4
                if j >= 0:
                    tp, _, hp, rows = na_step(j)
                    act.wait_ge(SN["pv"], j + 1)
                    nc.scalar.activation(grid_cols(xgh[rows, 4 + hp, :], tp),
                                         ps[rows, 3 + 3 * (j % 2), 0:2 * P].rearrange("p (c r) -> p c r", r=GRID_R),
                                         ACT.Copy).then_inc(SN["o_hi"], 1)
                if i in NA_SPLITS:
                    split_hi_part(act, *NA_SPLITS[i])
                if i < 4:
                    a = i
                    act.wait_ge(oan_done, a + 1)
                    act.wait_ge(w_half, 2 * (BE + 12))
                    nc.scalar.activation(xgh[:, a, :], oA[:, a, :], ACT.Copy).then_inc(mix_hi, 1)
                if 2 <= i < 16:
                    na_exp_act(act, i)

        def na_max_dve(dve, i):
            tp, h, _, _ = na_step(i)
            b = 2 * (i % 2)
            dve.wait_ge(bm_done, 2 if tp == 0 else 3 + h)
            dve.wait_ge(SN["scores"], 2 * i + 2)
            if i >= 2:
                dve.wait_ge(SN["exp"], 2 * (i - 1))
            both = slice(None) if tp == 0 else slice(None, None, -1)
            nc.vector.tensor_tensor(sB[:, i % 2, :, :], ps[:, 4 + i % 2, :].rearrange("p (s k) -> p s k", s=2),
                                    bm[:, both, h, :, :].rearrange("p s j c -> p s (j c)"),
                                    ALU.add).then_inc(SN["scores_read"], 1)
            dve.wait_ge(SN["scores_read"], i + 1)
            nc.vector.tensor_reduce(col(C_NMX + b, 2), sB[:, i % 2, :, :], AX, ALU.max,
                                    negate=True).then_inc(SN["max"], 1)

        def na_dve(dve):
            for i in range(20):
                if i >= 5 and i % 2:
                    wo_first_dve(dve, (i - 5) // 2)
                j = i - 1
                if 0 <= j < 16:
                    rec = recs[:, 2 * (j % 2):2 * (j % 2) + 2]
                    t = j // 8
                    dve.wait_ge(SN["exp"], 2 * j + 2)
                    if j >= 2:
                        dve.wait_ge(n_norm2, j - 1)
                        dve.wait_ge(n_norm, j - 1)
                    nc.vector.reciprocal(rec, col(C_SUM + 2 * (j % 2), 2)).then_inc(SN["rec"], 1)
                    dve.wait_ge(SN["rec"], j + 1)
                    nc.vector.tensor_scalar(na_window(j, t), na_window(j, t), rec[:, t:t + 1], None,
                                            ALU.mult).then_inc(n_norm, 1)
                if 2 <= i < 16:
                    na_max_dve(dve, i)
                j = i - 2
                if 0 <= j < 16:
                    for t in range(2):
                        z = 2 * j + t
                        kk = na_tile(j, t)[1]
                        n = kk.stop - kk.start
                        dve.wait_ge(SN["hi"], z + 1)
                        nc.vector.tensor_tensor(bTl[:, j % 2, kk, t * P:(t + 1) * P],
                                                ps[:, z % 3, 0:n * P].rearrange("p (k q) -> p k q", k=n),
                                                bTh[:, j % 2, kk, t * P:(t + 1) * P].bitcast(F32),
                                                ALU.subtract).then_inc(SN["lo"], 1)
                j = i - 4
                if j >= 0:
                    tp, _, hp, rows = na_step(j)
                    dve.wait_ge(SN["o_hi"], j + 1)
                    nc.vector.tensor_tensor(grid_cols(xgl[rows, 4 + hp, :], tp),
                                            ps[rows, 3 + 3 * (j % 2), 0:2 * P].rearrange("p (c r) -> p c r", r=GRID_R),
                                            grid_cols(xgh[rows, 4 + hp, :], tp).bitcast(F32),
                                            ALU.subtract).then_inc(SN["o_lo"], 1)
                if 1 <= i < 5:
                    a = i - 1
                    dve.wait_ge(mix_hi, a + 1)
                    nc.vector.tensor_tensor(xgl[:, a, :], oA[:, a, :], xgh[:, a, :].bitcast(F32),
                                            ALU.subtract).then_inc(mix_lo, 1)

        def bm_pool(pool, slot, kind, heads):
            t = (0, 1, 3)[kind]
            w0 = 47 - (WSTART[t] - 16 * t + 16)
            n = heads.stop - heads.start
            rel = relb[:, heads, ::-1, w0:(w0 - WIN if w0 >= WIN else None):-1]
            mk = mask[:, kind:kind + 1, :].broadcast_to([P, 8 * n, WIN])
            nc.gpsimd.tensor_tensor(bm[:, slot, heads, :, :], rel, mk.rearrange("p (h j) c -> p h j c", h=n),
                                    ALU.add).then_inc(bm_done, 1)

        def na_pool(pool):
            pool.wait_ge(mask_in, 65 * 16)
            pool.wait_ge(al_done, 16)
            pool.wait_ge(oa_done, 8)
            nc.gpsimd.memset(pN[:, :, 0:3 * P], 0.0).then_inc(pn_zero, 1)
            bm_pool(pool, 0, 0, slice(0, 8))
            bm_pool(pool, 1, 1, slice(0, 8))
            for j in range(16):
                t = 1 - j // 8
                pool.wait_ge(SN["rec"], j + 1)
                nc.gpsimd.tensor_tensor(na_window(j, t), na_window(j, t),
                                        recs[:, 2 * (j % 2) + t:2 * (j % 2) + t + 1].broadcast_to([P, 8 * WIN]),
                                        ALU.mult).then_inc(n_norm2, 1)
                if j in NA_SPLITS:
                    split_lo_part(pool, *NA_SPLITS[j])
                if j < 8:
                    pool.wait_ge(SN["scores_read"], j + 1)
                    bm_pool(pool, 0, 2, slice(j, j + 1))

        def mla_step(i):
            h, q0 = i // 2, 2 * P * (i % 2)
            return h, h // 2, slice(64 * (h % 2), 64 * (h % 2) + 64), q0

        def mla_bank(i):
            return 4 if i % 2 else 6

        def mla_scores_pe(pe, i):
            h, _, _, q0 = mla_step(i)
            for ready, n in ((qd_lo, h + 1), (kd_lo, h + 1), (kr_lo, h + 1)):
                pe.wait_ge(ready, n)
            if i >= 2:
                pe.wait_ge(SM["exp"], 2 * (i - 1))
            for t in range(2):
                q = [k[:, h, q0 + t * P:q0 + (t + 1) * P] for k in (qdh, qdl)]
                three(ps[:, mla_bank(i) + t, :], *q, kdh[:, h, :], kdl[:, h, :],
                      True, True).then_inc(SM["scores"], 1)

        def mla_pe(pe):
            for i in range(19):
                if i == 1:
                    pe.wait_ge(kd_lo, 8)
                if 1 <= i < 16:
                    mla_scores_pe(pe, i)
                j = i - 2
                if 0 <= j < 16:
                    if j == 0:
                        pe.wait_ge(vd_lo, 4)
                        pe.wait_ge(qd_lo, 8)
                        pe.wait_ge(kr_lo, 8)
                    for t in range(2):
                        z = 2 * j + t
                        if t == 0:
                            pe.wait_ge(m_norm, j + 1)
                        else:
                            pe.wait_ge(m_norm2, j + 1)
                        if z >= 3:
                            pe.wait_ge(SM["lo"], z - 2)
                        for k in range(TT):
                            mm = nc.tensor.transpose(ps[:, z % 3, k * P:(k + 1) * P],
                                                     eD[:, j % 2, t, k * P:(k + 1) * P], ident[:, :])
                        mm.then_inc(SM["turned"], 1)
                j = i - 3
                if 0 <= j < 16:
                    _, hp, _, _ = mla_step(j)
                    pe.wait_ge(SM["lo"], 2 * j + 2)
                    if j:
                        pe.wait_ge(SM["o"], j)
                    for k in range(TT):
                        mm = three(ps[:, 3, 0:2 * P], vdh[:, k, hp * P:(hp + 1) * P], vdl[:, k, hp * P:(hp + 1) * P],
                                   dTh[:, j % 2, k, :], dTl[:, j % 2, k, :], k == 0, k == TT - 1)
                    mm.then_inc(SM["pv"], 1)
                if i >= 17:
                    pe.wait_ge(SM["exp"], 32)
                    down_mixer_part(pe, U_WO, 0, i - 17, (4, 5, 6, 7), lambda k: (omix_lo, k + 1), {}, False)

        def mla_exp_act(act, i):
            act.wait_ge(SM["max"], i + 1)
            if i >= 2:
                act.wait_ge(SM["turned"], 2 * (i - 1))
            for t in range(2):
                c = 2 * (i % 2) + t
                nc.scalar.activation(eD[:, i % 2, t, :], ps[:, mla_bank(i) + t, :], ACT.Exp, bias=col(C_NMX + c),
                                     scale=MS, accum_out=col(C_SUM + c)).then_inc(SM["exp"], 1)

        def mla_act(act):
            for i in range(20):
                j = i - 4
                if j >= 0:
                    _, hp, rows, q0 = mla_step(j)
                    act.wait_ge(SM["pv"], j + 1)
                    nc.scalar.activation(oD[rows, hp, q0:q0 + 2 * P], ps[rows, 3, 0:2 * P],
                                         ACT.Copy).then_inc(SM["o"], 1)
                j = i - 2
                if 0 <= j < 16:
                    if j >= 2:
                        act.wait_ge(SM["pv"], j - 1)
                    for t in range(2):
                        z = 2 * j + t
                        act.wait_ge(SM["turned"], z + 1)
                        nc.scalar.activation(dTh[:, j % 2, :, t * P:(t + 1) * P],
                                             ps[:, z % 3, :].rearrange("p (k q) -> p k q", k=TT),
                                             ACT.Copy).then_inc(SM["hi"], 1)
                if 1 <= i < 16:
                    mla_exp_act(act, i)
                if 1 <= i < 9:
                    split_hi_part(act, U_WO + (i - 1) // 4, (i - 1) % 4, 2 + (i - 1) // 4)

        def mla_max_dve(dve, i):
            b = 2 * (i % 2)
            dve.wait_ge(SM["scores"], 2 * i + 2)
            nc.vector.tensor_reduce(col(C_CF + b, 2), ps[:, mla_bank(i):mla_bank(i) + 2, :], AX, ALU.max).then_inc(mxraw, 1)
            dve.wait_ge(mxraw, i + 1)
            nc.vector.tensor_scalar(col(C_NMX + b, 2), col(C_CF + b, 2), -MS, None,
                                    ALU.mult).then_inc(SM["max"], 1)

        def mla_dve(dve):
            for i in range(18):
                j = i - 1
                if 0 <= j < 16:
                    rec = recs[:, 2 * (j % 2):2 * (j % 2) + 2]
                    dve.wait_ge(SM["exp"], 2 * j + 2)
                    if j >= 2:
                        dve.wait_ge(m_norm2, j - 1)
                        dve.wait_ge(m_norm, j - 1)
                    nc.vector.reciprocal(rec, col(C_SUM + 2 * (j % 2), 2)).then_inc(SM["rec"], 1)
                    dve.wait_ge(SM["rec"], j + 1)
                    nc.vector.tensor_scalar(eD[:, j % 2, 0, :], eD[:, j % 2, 0, :], rec[:, 0:1], None,
                                            ALU.mult).then_inc(m_norm, 1)
                if 1 <= i < 16:
                    mla_max_dve(dve, i)
                j = i - 2
                if j >= 0:
                    for t in range(2):
                        z = 2 * j + t
                        dve.wait_ge(SM["hi"], z + 1)
                        nc.vector.tensor_tensor(dTl[:, j % 2, :, t * P:(t + 1) * P],
                                                ps[:, z % 3, :].rearrange("p (k q) -> p k q", k=TT),
                                                dTh[:, j % 2, :, t * P:(t + 1) * P].bitcast(F32),
                                                ALU.subtract).then_inc(SM["lo"], 1)

        def mla_pool(pool):
            pool.wait_ge(kr_lo, 8)
            for j in range(16):
                pool.wait_ge(SM["rec"], j + 1)
                nc.gpsimd.tensor_tensor(eD[:, j % 2, 1, :], eD[:, j % 2, 1, :],
                                        recs[:, 2 * (j % 2) + 1:2 * (j % 2) + 2].broadcast_to([P, SEQ]),
                                        ALU.mult).then_inc(m_norm2, 1)
                if 1 <= j < 9:
                    split_lo_part(pool, U_WO + (j - 1) // 4, (j - 1) % 4, 2 + (j - 1) // 4)

        def down_mixer_part(pe, B, j, k2, banks, split_done, gates, last):
            c = B + j
            s = c % 2
            pe.wait_ge(w_lo, c + 1)
            pe.wait_ge(*split_done(2 * j + k2))
            for b in banks:
                if b in gates:
                    pe.wait_ge(*gates[b])
                o = k2 * D + b * P
                mm = three(ps[:, b, :], wh[:, s, o:o + P], wl[:, s, o:o + P],
                           xgh[:, 2 * j + k2, :], xgl[:, 2 * j + k2, :], j == 0 and k2 == 0, False)
            if last:
                mm.then_inc(w_half, last)

        def down_mixer_pe(pe, B, split_done, gates):
            for k2 in range(2):
                down_mixer_part(pe, B, 0, k2, range(4), split_done, {} if k2 else gates, 2 * k2)
            for j in (1, 2):
                for k2 in range(2):
                    down_mixer_part(pe, B, j, k2, range(KD), split_done, {}, 1)
            pe.wait_ge(*split_done(7))
            down_last_pe(pe, B + 3, 6, xgh, xgl)

        def even_load(act):
            act.wait_ge(x_new, 8)
            for dst, src in ((cosA, rope_a[0:P, :]), (sinA, rope_a[P:2 * P, :]), (permA, perm_d[:, 0:P])):
                act.dma_start(dst[:, :], src).then_inc(even_in, 16)
            act.dma_start(lamb, lamvec.partition_broadcast(P)).then_inc(even_in, 16)

        def even_load_bias(sp):
            sp.wait_ge(ssum_done, 2)
            sp.dma_start(mask, masks_d.rearrange("p (m c) -> p m c", m=3)).then_inc(mask_in, 16)
            for h in range(8):
                for j in range(8):
                    src = bass.AP(tensor=rpb.tensor, offset=960 * h + 64 * j, ap=[[1, 16], [64, 8], [1, 48]])
                    sp.dma_start(relb[:, h, j, :], src).then_inc(mask_in, 16)

        def even_pe(pe):
            for i in range(8):
                c = BE + i // 2
                pe.wait_ge(w_lo, c + 1)
                if i >= 2:
                    pe.wait_ge(q32_done, i - 1)
                block_T(pe, ps[:, i % 2, :], c, i % 2, wait_x=8 if i == 0 else None).then_inc(w_half, 1)
                if i == 0:
                    norm_pe(pe, 1, 4)
                    pe.wait_ge(even_in, 64)
                else:
                    rot_pe(pe, i - 1)
                if i == 1:
                    norm_reads_pe(pe)
            for v in range(2):
                c = BE + 4 + v
                pe.wait_ge(w_lo, c + 1)
                for t in range(TT):
                    if v == 0 and t == 0:
                        pe.wait_ge(rcol_read, 1)
                    if v == 1:
                        pe.wait_ge(va_lo, t + 1)
                    mm = block_V(ps[:, 4 + t, 0:256], c, lambda b, k, t=t: b[:, k, t * P:(t + 1) * P], 256, 256)
                    if t % 2:
                        mm.then_inc(w_half, 1)
                    if v == 0 and t == 0:
                        rot_pe(pe, 7)
                if v == 0:
                    pe.wait_ge(qa_lo, 8)
                    diff_scores_pe(pe, 0)
                    diff_scores_pe(pe, 1)
            diff_pe(pe)
            for i in range(1, 13):
                if i < 12:
                    na_block_pe(pe, i)
                if i == 10:
                    pe.wait_ge(qb_lo, 8)
                    pe.wait_ge(arms_done, 4)
                    na_scores_pe(pe, 0)
                    na_scores_pe(pe, 1)
                if i in (2, 3, 6, 7):
                    a = (2, 3, 6, 7).index(i)
                    if i == 2:
                        pe.wait_ge(al_done, 16)
                        pe.wait_ge(oa_done, 8)
                    diff_norm_pe(pe, a)
                j = i - 1
                if j >= 8:
                    pe.wait_ge(qb32_done, j + 1)
                    if j >= 10:
                        pe.wait_ge(vb_lo, j - 9)
                    for t in range(TT):
                        mm = nc.tensor.transpose(ps[:, 2 + j % 2, t * P:(t + 1) * P],
                                                 qb32[:, j % 2, t * P:(t + 1) * P], ident[:, :])
                    mm.then_inc(vt_done, 1)
            na_pe(pe)
            wo_second_pe(pe)

        def even_act(act):
            even_load(act)
            for i in range(8):
                c = BE + i // 2
                if i % 2 == 0:
                    split_hi(act, c + 1)
                if i == 0:
                    norm_act(act, 1, 4)
                    act.wait_ge(even_in, 64)
                if i == 1:
                    act.wait_ge(lam_done, 2)
                    nc.scalar.activation(col(C_LAM, 2), col(C_LAM, 2), ACT.Exp).then_inc(lam_exp, 1)
                if i >= 1:
                    qa_hi_act(act, i - 1)
            split_hi(act, BE + 5)
            qa_hi_act(act, 7)
            for v in range(2):
                c = BE + 4 + v
                if v:
                    split_hi(act, c + 1)
                for t in range(TT):
                    act.wait_ge(w_half, 2 * c + t // 2 + 1)
                    act.wait_ge(rcol_read, 1)
                    nc.scalar.activation(vah[:, t, v * 256:v * 256 + 256], ps[:, 4 + t, 0:256], ACT.Copy,
                                         scale=col(C_RN + t)).then_inc(va_hi, 1)
                if v == 0:
                    diff_exp_act(act, 0)
                    diff_exp_act(act, 1)
            diff_act(act)
            diff_norm_act(act, 0)
            for i in range(12):
                c = BE + 6 + i // 2
                if i and i % 2 == 0:
                    split_hi(act, c + 1)
                if i in (4, 8):
                    diff_sqrt_act(act, i // 2 - 2)
                if i == 6:
                    diff_norm_act(act, 2)
                if i == 11:
                    na_exp_act(act, 0)
                    na_exp_act(act, 1)
                if i < 8:
                    dst = (qbh if i < 4 else kbh)[:, i % 4, :]
                    act.wait_ge(qb32_done, i + 1)
                    nc.scalar.activation(dst, qb32[:, i % 2, :], ACT.Copy).then_inc(qb_hi, 1)
                else:
                    f = i - 8
                    act.wait_ge(vt_done, f + 1)
                    nc.scalar.activation(vbh[:, :, f * P:(f + 1) * P],
                                         ps[:, 2 + i % 2, :].rearrange("p (t f) -> p t f", t=TT),
                                         ACT.Copy).then_inc(vb_hi, 1)
            na_act(act)
            split_hi(act, BE + 15)
            finish_act(act, 2, BE + 15, held=4, split=BE + 16)

        def qa_hi_act(act, i):
            dst = (qah if i < 4 else kah)[:, i % 4, :]
            act.wait_ge(qr_done, i + 1)
            nc.scalar.activation(dst, qs[:, i % 2, :], ACT.Copy, scale=QS if i < 4 else 1.0).then_inc(qa_hi, 1)

        def even_dve(dve):
            dve.wait_ge(even_in, 64)
            nc.vector.tensor_tensor(lamp, lamb.rearrange("p (a b e) -> p a b e", a=2, b=2)[:, :, 0, :],
                                    lamb.rearrange("p (a b e) -> p a b e", a=2, b=2)[:, :, 1, :],
                                    ALU.mult).then_inc(lam_done, 1)
            dve.wait_ge(lam_done, 1)
            nc.vector.tensor_reduce(col(C_LAM, 2), lamp, AX, ALU.add).then_inc(lam_done, 1)
            for i in range(8):
                c = BE + i // 2
                if i % 2 == 0:
                    split_lo(dve, c + 1)
                if i == 0:
                    norm_dve(dve, 1)
                    dve.wait_ge(rstd, 2)
                dve.wait_ge(w_half, 2 * c + i % 2 + 1)
                if i >= 2:
                    dve.wait_ge(qc_done, i - 1)
                nc.vector.tensor_tensor(q32[:, i % 2, :], ps[:, i % 2, :], rB[:, :], ALU.mult).then_inc(q32_done, 1)
                if i >= 1:
                    qa_dve(dve, i - 1)
                if i == 3:
                    dve.wait_ge(lam_exp, 1)
                    nc.vector.scalar_tensor_tensor(col(C_NLAM), col(C_LAM + 1), -LAM_INIT, col(C_LAM),
                                                   ALU.add, ALU.subtract).then_inc(lam_done, 1)
                    nc.vector.tensor_scalar(vec(V_SUB), vec(V_SUB), 1.0 - LAM_INIT, None,
                                            ALU.mult).then_inc(lam_done, 1)
                    dve.wait_ge(rcol_done, 1)
                    nc.vector.tensor_copy(col(C_RN, 4), ps[:, 5, 0:4]).then_inc(rcol_read, 1)
            split_lo(dve, BE + 5)
            qa_dve(dve, 7)
            for v in range(2):
                c = BE + 4 + v
                if v:
                    split_lo(dve, c + 1)
                for t in range(TT):
                    dve.wait_ge(va_hi, 4 * v + t + 1)
                    nc.vector.scalar_tensor_tensor(val[:, t, v * 256:v * 256 + 256], ps[:, 4 + t, 0:256],
                                                   col(C_RN + t), vah[:, t, v * 256:v * 256 + 256].bitcast(F32),
                                                   ALU.mult, ALU.subtract).then_inc(va_lo, 1)
                    if v == 1 and t == 0:
                        dve.wait_ge(lam_done, 4)
                        diff_rec_dve(dve, 0)
                    if v == 1 and t == 2:
                        diff_comb_dve(dve, 0)
                if v == 0:
                    diff_max_dve(dve, 0)
                    diff_max_dve(dve, 1)
            diff_dve(dve)
            for i in range(12):
                c = BE + 6 + i // 2
                if i and i % 2 == 0:
                    split_lo(dve, c + 1)
                if i == 11:
                    na_max_dve(dve, 0)
                    na_max_dve(dve, 1)
                dve.wait_ge(w_half, 2 * c + i % 2 + 1)
                if 2 <= i < 10:
                    dve.wait_ge(qb_lo, i - 1)
                elif i >= 10:
                    dve.wait_ge(vt_done, i - 9)
                if i < 4 or i >= 8:
                    nc.vector.scalar_tensor_tensor(qb32[:, i % 2, :].rearrange("p (c r) -> p r c", r=GRID_R),
                                                   ps[:, i % 2, :].rearrange("p (r c) -> p r c", r=GRID_R),
                                                   QS if i < 4 else 1.0,
                                                   rB[:, :].rearrange("p (r c) -> p r c", r=GRID_R),
                                                   ALU.mult, ALU.mult).then_inc(qb32_done, 1)
                else:
                    nc.vector.tensor_tensor(qb32[:, i % 2, :], ps[:, i % 2, :], rB[:, :],
                                            ALU.mult).then_inc(qb32_done, 1)
                if i < 8:
                    dve.wait_ge(qb_hi, i + 1)
                    hi, lo = (t_[:, i % 4, :] for t_ in ((qbh, qbl) if i < 4 else (kbh, kbl)))
                    nc.vector.tensor_tensor(lo, qb32[:, i % 2, :], hi.bitcast(F32), ALU.subtract).then_inc(qb_lo, 1)
                if i in (4, 5, 8, 9):
                    diff_norm_dve(dve, (4, 5, 8, 9).index(i))
                if i >= 9:
                    vb_lo_dve(dve, i - 1)
            vb_lo_dve(dve, 11)
            na_dve(dve)
            dve.wait_ge(w_lo, BE + 15)
            split_lo(dve, BE + 15)
            finish_dve(dve, 2, 1.0, BE + 15, held=4, split=BE + 16)

        def vb_lo_dve(dve, i):
            f = i - 8
            dve.wait_ge(vb_hi, f + 1)
            nc.vector.tensor_tensor(vbl[:, :, f * P:(f + 1) * P],
                                    ps[:, 2 + i % 2, :].rearrange("p (t f) -> p t f", t=TT),
                                    vbh[:, :, f * P:(f + 1) * P].bitcast(F32), ALU.subtract).then_inc(vb_lo, 1)

        def qa_dve(dve, i):
            dve.wait_ge(rot_done, i + 1)
            if i >= 2:
                dve.wait_ge(qa_lo, i - 1)
            nc.vector.tensor_tensor(qs[:, i % 2, :], ps[:, 2 + i % 2, :], sinA[:, :], ALU.mult).then_inc(qs_done, 1)
            dve.wait_ge(qc_done, i + 1)
            dve.wait_ge(qs_done, i + 1)
            nc.vector.tensor_tensor(qs[:, i % 2, :], qs[:, i % 2, :], qc[:, i % 2, :], ALU.add).then_inc(qr_done, 1)
            dve.wait_ge(qa_hi, i + 1)
            hi, lo = (t_[:, i % 4, :] for t_ in ((qah, qal) if i < 4 else (kah, kal)))
            nc.vector.scalar_tensor_tensor(lo, qs[:, i % 2, :], QS if i < 4 else 1.0, hi.bitcast(F32),
                                           ALU.mult, ALU.subtract).then_inc(qa_lo, 1)

        def even_pool(pool):
            pool.wait_ge(even_in, 64)
            for i in range(8):
                pool.wait_ge(q32_done, i + 1)
                if i >= 2:
                    pool.wait_ge(qr_done, i - 1)
                nc.gpsimd.tensor_tensor(qc[:, i % 2, :], q32[:, i % 2, :], cosA[:, :], ALU.mult).then_inc(qc_done, 1)
            diff_pool(pool)
            na_pool(pool)
            finish_pool(pool, 2)

        BO = U_ODD
        MS = 96 ** -0.5
        INB = ([(BO + i // 2, i % 2, P) for i in range(4)] + [(BO + 2, 0, P), (BO + 2, 1, P), (BO + 3, 0, P),
               (BO + 3, 1, 96)] + [(BO + 5 + i // 2, i % 2, P) for i in range(4)])
        N_IN = len(INB)
        U_GATE, U_UQ, U_UKV, U_WO = BO + 4, BO + 7, BO + 8, BO + 9

        def odd_block_pe(pe, i):
            c, m, rows = INB[i]
            pe.wait_ge(w_lo, c + 1)
            if i >= 4:
                pe.wait_ge(in_read, i - 3)
            if i in (8, 9):
                pe.wait_ge(cstd_done, i - 7)
            block_T(pe, ps[0:rows, i % 4, :], c, m, width=rows,
                    wait_x=32 if i == 0 else None).then_inc(w_half, 1)

        def odd_pe(pe):
            odd_block_pe(pe, 0)
            norm_pe(pe, 4, 4)
            for i in range(1, 8):
                odd_block_pe(pe, i)
            pe.wait_ge(csq_sum, 1)
            pe.wait_ge(in_read, 6)
            pe.wait_ge(std_done, 5)
            nc.tensor.matmul(ps[:, 0, :], ones[:, :], sqt[:, 1, :], start=True, stop=True).then_inc(cs_done, 1)
            pe.wait_ge(csq_done, 3)
            nc.tensor.matmul(ps[:, 1, :], ones[:, :], acc[:, :], start=True, stop=True).then_inc(cs_done, 1)
            pe.wait_ge(w_lo, U_GATE + 1)
            s = U_GATE % 2
            for g in range(8):
                c, d = g // 2, g % 2
                if d == 0:
                    pe.wait_ge(u_lo, c + 1)
                if g >= 2:
                    pe.wait_ge(sig_done, 2 * (g - 1))
                for kind in range(2):
                    o = (d * 8 + kind * 4 + c) * P
                    mm = three(ps[:, 4 + 2 * (g % 2) + kind, :], wh[:, s, o:o + P], wl[:, s, o:o + P],
                               uh[:, c, :], ul[:, c, :], True, True)
                    if g < 7 or kind == 0:
                        mm.then_inc(gate_done, 1)
                    else:
                        mm.then_inc(w_half, 2)
            for i in range(8, N_IN):
                odd_block_pe(pe, i)
            pe.wait_ge(odd_in, 48)
            pe.wait_ge(w_lo, U_UKV + 1)
            pe.wait_ge(cq_lo, 3)
            pe.wait_ge(in_read, N_IN)
            pe.wait_ge(sig_done, 16)
            sq, sk = U_UQ % 2, U_UKV % 2
            for t in range(TT):
                if t >= 2:
                    pe.wait_ge(vd_lo, t - 1)
                wv = [w_[:, sk, 0:1024].rearrange("p (h e) -> p h e", h=8)[:, :, 64:128] for w_ in (wh, wl)]
                three(ps[:, 6 + t % 2, :], cqh[:, 2, t * P:(t + 1) * P], cql[:, 2, t * P:(t + 1) * P],
                      *wv, True, True).then_inc(vd_ps, 1)
            rotd_pe(pe, 0)
            for h in range(8):
                if h >= 2:
                    pe.wait_ge(qd32_done, h)
                for k in range(2):
                    o = k * 768 + h * 96
                    mm = three(ps[0:96, h % 2, :], wh[:, sq, o:o + 96], wl[:, sq, o:o + 96],
                               cqh[:, k, :], cql[:, k, :], k == 0, k == 1)
                mm.then_inc(*((qd_ps, 1) if h < 7 else (w_half, 2)))
                if h >= 2:
                    pe.wait_ge(kd_lo, h - 1)
                three(ps[:, 4 + h % 2, :], wh[:, sk, h * P:(h + 1) * P], wl[:, sk, h * P:(h + 1) * P],
                      cqh[:, 2, :], cql[:, 2, :], True, True).then_inc(*((kd_ps, 1) if h < 7 else (w_half, 2)))
                rotd_pe(pe, h + 1)
                if h == 6:
                    pe.wait_ge(vd_lo, 4)
                    mla_scores_pe(pe, 0)
            mla_pe(pe)
            down_mixer_pe(pe, U_WO, lambda k: (omix_lo, k + 1), {0: (SM["lo"], 32), 3: (SM["o"], 16)})

        def rotd_pe(pe, i):
            pe.wait_ge(qd32_done, i + 1)
            if i >= 2:
                pe.wait_ge(qds_done, i - 1)
            nc.tensor.matmul(ps[0:96, 2 + i % 2, :], permD[:, :], qd32[:, i % 2, :],
                             start=True, stop=True).then_inc(rotd_done, 1)

        def odd_act(act):
            def u_hi_act(k):
                act.wait_ge(u_done, 4 * k + 4)
                nc.scalar.activation(uh[:, k, :], u32[:, k, :], ACT.Copy).then_inc(u_hi, 1)

            split_hi(act, BO + 1)
            norm_act(act, 4, 4)
            split_hi(act, BO + 2)
            split_hi(act, BO + 3)
            u_hi_act(0)
            split_hi(act, U_GATE)
            u_hi_act(1)
            u_hi_act(2)
            act.wait_ge(in_read, 7)
            act.wait_ge(std_done, 5)
            act.wait_ge(rstd, 5)
            act.wait_ge(ssum_done, 5)
            nc.scalar.activation(sqt[:, 0, :], cq[:, 0, :], ACT.Square).then_inc(csq_done, 1)
            nc.scalar.activation(sqt[:, 1, :], cq[:, 1, :], ACT.Square).then_inc(csq_done, 1)
            nc.scalar.activation(acc[:, :], cq[:, 2, :], ACT.Square).then_inc(csq_done, 1)
            split_hi(act, U_GATE + 1)
            for z, n in enumerate((256, 128)):
                act.wait_ge(cs_done, 2)
                nc.scalar.activation(sqt[:, z, :], ps[:, z, :], ACT.Sqrt, bias=col(C_EPS),
                                     scale=1.0 / n).then_inc(cstd_done, 1)
            u_hi_act(3)
            for g in range(8):
                c, d = g // 2, g % 2
                for kind in range(2):
                    act.wait_ge(gate_done, 2 * g + kind + 1) if (g, kind) != (7, 1) else                         act.wait_ge(w_half, 2 * (U_GATE + 1))
                    dst = (ra, iu)[kind][:, g, :]
                    nc.scalar.activation(dst, ps[:, 4 + 2 * (g % 2) + kind, :], ACT.Sigmoid,
                                         bias=vec((V_BA, V_BX)[kind] + 4 * d + c)).then_inc(sig_done, 1)
            split_hi(act, U_GATE + 2)
            for g in range(8):
                c, d = g // 2, g % 2
                act.wait_ge(sig_done, 2 * g + 1)
                nc.scalar.activation(th[:, g, :], ra[:, g, :], ACT.Tanh, scale=col(C_P8 + 4 * d + c)).then_inc(th_done, 1)
            for g in range(8):
                c, d = g // 2, g % 2
                act.wait_ge(th_done, g + 1)
                nc.scalar.activation(ra[:, g, :], ra[:, g, :], ACT.Exp, scale=col(C_M8 + 4 * d + c)).then_inc(a_done, 1)
            for g in range(8):
                act.wait_ge(vv_done, g + 1)
                nc.scalar.activation(th[:, g, :], th[:, g, :], ACT.Sqrt).then_inc(mult_done, 1)
            split_hi(act, U_UQ, n=1536)
            for c in range(4):
                act.wait_ge(in_read, 9 + c)
                nc.scalar.activation(gc[:, c, :], gc[:, c, :], ACT.Gelu_apprx_tanh).then_inc(gelu_done, 1)
            split_hi(act, U_UKV, n=1024)
            for c in range(4):
                act.wait_ge(oc_done, c + 1)
                nc.scalar.activation(xgh[:, c, :], gc[:, c, :], ACT.Copy).then_inc(omix_hi, 1)
            vd_hi_act(act, 0)
            vd_hi_act(act, 1)
            for i in range(10):
                if i == 0:
                    act.wait_ge(omix_lo, 4)
                    nc.scalar.activation(qd32[:, 0, :], kpe[:, :], ACT.Copy).then_inc(qd32_done, 1)
                elif i < 9:
                    act.wait_ge(qd_ps, i) if i < 8 else act.wait_ge(w_half, 2 * (U_UQ + 1))
                    if i >= 2:
                        act.wait_ge(qdc_done, i - 1)
                        act.wait_ge(rotd_done, i - 1)
                    nc.scalar.activation(qd32[:, i % 2, :], ps[0:96, (i - 1) % 2, :], ACT.Copy).then_inc(qd32_done, 1)
                h = i - 1
                if 0 <= h < 8:
                    act.wait_ge(kd_ps, h + 1) if h < 7 else act.wait_ge(w_half, 2 * (U_UKV + 1))
                    nc.scalar.activation(kdh[0:64, h, :], ps[0:64, 4 + h % 2, :], ACT.Copy).then_inc(kd_hi, 1)
                if i == 9:
                    mla_exp_act(act, 0)
                if i >= 2:
                    qd_hi_act(act, i - 1)
                if i >= 1 and i < 9:
                    act.wait_ge(qdr_done, 1)
                    nc.scalar.activation(kdh[64:96, i - 1, :], kpe[64:96, :], ACT.Copy).then_inc(kr_hi, 1)
                if i == 0:
                    vd_hi_act(act, 2)
                    vd_hi_act(act, 3)
            mla_act(act)
            for k in range(4):
                act.wait_ge(SM["o"], 4 * k + 4)
                if k == 0:
                    act.wait_ge(SM["pv"], 16)
                nc.scalar.activation(xgh[:, 4 + k, :], oD[:, k, :], ACT.Copy).then_inc(omix_hi, 1)
            for j in range(2, 5):
                split_hi(act, U_WO + j)
            finish_act(act, 5, U_WO + 3)

        def vd_hi_act(act, t):
            act.wait_ge(vd_ps, t + 1)
            nc.scalar.activation(vdh[:, t, :], ps[:, 6 + t % 2, :], ACT.Copy).then_inc(vd_hi, 1)

        def qd_hi_act(act, i):
            act.wait_ge(qdr_done, i + 1)
            nc.scalar.activation(qdh[:, i - 1, :], qds[:, i % 2, :], ACT.Copy).then_inc(qd_hi, 1)

        def odd_dve(dve):
            def evac(i):
                c, m, rows = INB[i]
                dst = (xcp[:, i, 1:SEQ + 1] if i < 4 else cq[:, i - 4, :] if i < 7 else kpe[:, :] if i == 7
                       else gc[:, i - 8, :])
                dve.wait_ge(w_half, 2 * c + m + 1)
                nc.vector.tensor_tensor(dst, ps[0:rows, i % 4, :], rB[0:rows, :], ALU.mult).then_inc(in_read, 1)

            def u_lo_dve(k):
                dve.wait_ge(u_hi, k + 1)
                nc.vector.tensor_tensor(ul[:, k, :], u32[:, k, :], uh[:, k, :].bitcast(F32),
                                        ALU.subtract).then_inc(u_lo, 1)

            split_lo(dve, BO + 1)
            nc.vector.memset(xcp[:, :, 0:1], 0.0).then_inc(pad_done, 1)
            nc.vector.memset(xcp[:, :, SEQ + 1:SEQ + 3], 0.0).then_inc(pad_done, 1)
            norm_dve(dve, 4)
            dve.wait_ge(rstd, 5)
            evac(0)
            evac(1)
            split_lo(dve, BO + 2)
            evac(2)
            evac(3)
            for i in range(4, 8):
                if i % 2 == 0:
                    split_lo(dve, BO + i // 2 + 1)
                evac(i)
                conv_dve(dve, i - 4)
                if i > 4:
                    u_lo_dve(i - 5)
            split_lo(dve, U_GATE + 1)
            u_lo_dve(3)
            for z in range(2):
                dve.wait_ge(cstd_done, z + 1)
                nc.vector.reciprocal(sqt[:, z, :], sqt[:, z, :]).then_inc(crs_done, 1)
            for k in range(3):
                dve.wait_ge(crs_done, k // 2 + 1)
                nc.vector.scalar_tensor_tensor(cq[:, k, :], cq[:, k, :], vec(V_GQ + k), sqt[:, k // 2, :],
                                               ALU.mult, ALU.mult).then_inc(cqn_done, 1)
            for k in range(3):
                dve.wait_ge(cqn_done, k + 1)
                nc.vector.tensor_copy(cqh[:, k, :], cq[:, k, :]).then_inc(cq_hi, 1)
            for k in range(3):
                dve.wait_ge(cq_hi, k + 1)
                nc.vector.tensor_tensor(cql[:, k, :], cq[:, k, :], cqh[:, k, :].bitcast(F32),
                                        ALU.subtract).then_inc(cq_lo, 1)
            split_lo(dve, U_GATE + 2)
            for g in range(8):
                dve.wait_ge(th_done, g + 1)
                nc.vector.tensor_scalar(th[:, g, :], th[:, g, :], 2.0 ** -115, None, ALU.max).then_inc(tmax_done, 1)
            evac(8)
            for g in range(8):
                if g % 2:
                    dve.wait_ge(a_done, g + 1)
                    if g >= 4:
                        dve.wait_ge(vv_done, g - 3)
                    nc.vector.tensor_tensor(sq_of(g), ra[:, g, :], ra[:, g, :], ALU.mult).then_inc(asqo_done, 1)
                    dve.wait_ge(asqo_done, g // 2 + 1)
                else:
                    dve.wait_ge(asq_done, g // 2 + 1)
                dve.wait_ge(tmax_done, g + 1)
                nc.vector.scalar_tensor_tensor(th[:, g, :], sq_of(g), 1.0, th[:, g, :],
                                               ALU.add, ALU.mult).then_inc(vv_done, 1)
                if g == 5:
                    evac(9)
            evac(10)

            def mix_lo_dve(c):
                dve.wait_ge(omix_hi, c + 1)
                nc.vector.tensor_tensor(xgl[:, c, :], gc[:, c, :], xgh[:, c, :].bitcast(F32),
                                        ALU.subtract).then_inc(omix_lo, 1)

            for c in range(4):
                for g in (2 * c, 2 * c + 1):
                    rev = slice(None, None, -1) if g % 2 else slice(None)
                    dve.wait_ge(bt_done, g + 1)
                    nc.vector.tensor_tensor_scan(th[:, g, rev], ra[:, g, rev], iu[:, g, rev], 0.0,
                                                 ALU.mult, ALU.add).then_inc(h_done, 1)
                if c == 0:
                    evac(11)
                    split_lo(dve, U_UQ, n=1536)
                if c:
                    mix_lo_dve(c - 1)
                dve.wait_ge(h_done, 2 * c + 2)
                nc.vector.tensor_tensor(th[:, g, :], th[:, g, :], th[:, g - 1, :], ALU.add).then_inc(hs_done, 1)
                dve.wait_ge(hs_done, c + 1)
                dve.wait_ge(gelu_done, c + 1)
                nc.vector.tensor_tensor(gc[:, c, :], gc[:, c, :], th[:, g, :], ALU.mult).then_inc(oc_done, 1)
            split_lo(dve, U_UKV, n=1024)
            mix_lo_dve(3)
            def vd_lo_dve(t):
                dve.wait_ge(vd_hi, t + 1)
                nc.vector.tensor_tensor(vdl[:, t, :], ps[:, 6 + t % 2, :], vdh[:, t, :].bitcast(F32),
                                        ALU.subtract).then_inc(vd_lo, 1)

            for t in range(TT):
                vd_lo_dve(t)
            for i in range(9):
                if i == 8:
                    mla_max_dve(dve, 0)
                dve.wait_ge(odd_in, 48)
                dve.wait_ge(rotd_done, i + 1)
                if i >= 3:
                    dve.wait_ge(qd_lo, i - 2)
                nc.vector.tensor_tensor(qds[:, i % 2, :], ps[0:96, 2 + i % 2, :], sinD[:, :],
                                        ALU.mult).then_inc(qds_done, 1)
                dve.wait_ge(qdc_done, i + 1)
                dve.wait_ge(qds_done, i + 1)
                nc.vector.tensor_tensor(qds[:, i % 2, :] if i else kpe[:, :], qds[:, i % 2, :], qdc[:, i % 2, :],
                                        ALU.add).then_inc(qdr_done, 1)
                h = i - 1
                if h >= 0:
                    dve.wait_ge(kd_hi, h + 1)
                    nc.vector.tensor_tensor(kdl[0:64, h, :], ps[0:64, 4 + h % 2, :], kdh[0:64, h, :].bitcast(F32),
                                            ALU.subtract).then_inc(kd_lo, 1)
                if i:
                    dve.wait_ge(qd_hi, i)
                    nc.vector.tensor_tensor(qdl[:, i - 1, :], qds[:, i % 2, :], qdh[:, i - 1, :].bitcast(F32),
                                            ALU.subtract).then_inc(qd_lo, 1)
            mla_dve(dve)
            for k in range(4):
                dve.wait_ge(omix_hi, 4 + k + 1)
                nc.vector.tensor_tensor(xgl[:, 4 + k, :], oD[:, k, :], xgh[:, 4 + k, :].bitcast(F32),
                                        ALU.subtract).then_inc(omix_lo, 1)
            dve.wait_ge(w_lo, U_WO + 2)
            for j in range(2, 5):
                split_lo(dve, U_WO + j)
            finish_dve(dve, 5, 1.0, U_WO + 3)

        def sq_of(g):
            return xcp[:, g % 4, 0:SEQ]

        def conv_dve(dve, k):
            dve.wait_ge(in_read, k + 1)
            dve.wait_ge(pad_done, 2)
            for j in range(4):
                if j == 0:
                    ins = nc.vector.tensor_scalar(u32[:, k, :], xcp[:, k, 0:SEQ], vec(V_CW + k), vec(V_CB + k),
                                                  ALU.mult, ALU.add)
                else:
                    dve.wait_ge(u_done, 4 * k + j)
                    ins = nc.vector.scalar_tensor_tensor(u32[:, k, :], xcp[:, k, j:j + SEQ], vec(V_CW + 4 * j + k),
                                                         u32[:, k, :], ALU.mult, ALU.add)
                ins.then_inc(u_done, 1)

        def odd_pool(pool):
            pool.wait_ge(x_new, 8 * 4)
            for dst, src in ((cosD, rope_d[0:96, :]), (sinD, rope_d[96:192, :]), (permD, perm_d[0:96, P:P + 96])):
                pool.dma_start(dst[:, :], src).then_inc(odd_in, 16)
            pool.wait_ge(csq_done, 2)
            nc.gpsimd.tensor_tensor(sqt[:, 1, :], sqt[:, 0, :], sqt[:, 1, :], ALU.add).then_inc(csq_sum, 1)
            for g in range(8):
                pool.wait_ge(sig_done, 2 * g + 2)
                nc.gpsimd.tensor_tensor(iu[:, g, :], iu[:, g, :], u32[:, g // 2, :], ALU.mult).then_inc(iu_done, 1)
            for g in range(0, 8, 2):
                pool.wait_ge(a_done, g + 1)
                if g >= 4:
                    pool.wait_ge(vv_done, g - 3)
                nc.gpsimd.tensor_tensor(sq_of(g), ra[:, g, :], ra[:, g, :], ALU.mult).then_inc(asq_done, 1)
            for g in range(8):
                first = SEQ - 1 if g % 2 else 0
                pool.wait_ge(mult_done, g + 1)
                nc.gpsimd.memset(th[:, g, first:first + 1], 1.0).then_inc(one_done, 1)
                pool.wait_ge(one_done, g + 1)
                nc.gpsimd.tensor_tensor(iu[:, g, :], iu[:, g, :], th[:, g, :], ALU.mult).then_inc(bt_done, 1)
            pool.wait_ge(odd_in, 48)
            for i in range(9):
                pool.wait_ge(qd32_done, i + 1)
                if i >= 2:
                    pool.wait_ge(qdr_done, i - 1)
                    pool.wait_ge(kr_lo, i - 1)
                nc.gpsimd.tensor_tensor(qdc[:, i % 2, :], qd32[:, i % 2, :], cosD[:, :], ALU.mult).then_inc(qdc_done, 1)
                if i:
                    pool.wait_ge(kr_hi, i)
                    pool.wait_ge(qdc_done, i + 1)
                    nc.gpsimd.tensor_tensor(kdl[64:96, i - 1, :], kpe[64:96, :], kdh[64:96, i - 1, :].bitcast(F32),
                                            ALU.subtract).then_inc(kr_lo, 1)
            mla_pool(pool)
            finish_pool(pool, 5)


        block = ctx.enter_context(nc.Block())

        @block.sync
        def _(sp):
            for u in range(2):
                if u == 1:
                    sp.wait_ge(x_in[KD // 2], 16)
                sp.dma_start(raw[:, u, :], units[u * P:(u + 1) * P, :]).then_inc(raw_in[u], 16)

            def load(c, p):
                sp.wait_ge(w_lo, 2 * p + c - 1)
                sp.dma_start(raw[:, c % 2, :], units[bass.ds((c + 2 * p) * P, P), :]).then_inc(raw_in[c % 2], 16)

            for p0, p1 in ((0, (BE + 6) // 2 + 1), ((BE + 6) // 2 + 1, (N_UNITS - 2) // 2)):
                with sp.Fori(p0, p1) as p:
                    load(2, p)
                    load(3, p)
                if p0 == 0:
                    even_load_bias(sp)
            if N_UNITS % 2:
                load(N_UNITS - 1, 0)
            for b in range(KD):
                sp.wait_ge(out_done, b + 1)
                sp.dma_start(out[b * P:(b + 1) * P, :], x[:, b, :]).then_inc(stored, 16)
            sp.wait_ge(stored, 16 * KD)

        @block.gpsimd
        def _(pool):
            nc.gpsimd.memset(ones[:, :], 1.0).then_inc(ones_set, 1)
            finish_pool(pool, 0)
            ffn_pool(pool, 0, 0)
            even_pool(pool)
            ffn_pool(pool, 1, 2)
            ffn_pool(pool, 2, 3)
            odd_pool(pool)
            ffn_pool(pool, 3, 5)

        @block.tensor
        def _(pe):
            pe.wait_ge(ones_set, 1)
            ffn_pe(pe, 0, U_FFN[0], 0)
            even_pe(pe)
            ffn_pe(pe, 1, U_FFN[1], 2)
            ffn_pe(pe, 2, U_FFN[2], 3)
            odd_pe(pe)
            ffn_pe(pe, 3, U_FFN[3], 5)
            norm_pe(pe, 6, 0)

        @block.scalar
        def _(act):
            act.dma_start(gain[:, :], gains).then_inc(gain_in, 16)
            for b in range(KD):
                act.dma_start(x[:, b, :], xT[b * P:(b + 1) * P, :]).then_inc(x_in[b], 16)
            act.dma_start(cvec[:, :], colvec).then_inc(const_in, 16)
            act.dma_start(small[:, :], consts).then_inc(const_in, 16)
            act.dma_start(ident[:, :], ident_d).then_inc(const_in, 16)
            act.wait_ge(gain_in, 16)
            split_hi(act, 0)
            finish_act(act, 0)
            act.wait_ge(const_in, 48)
            setup_act(act)
            ffn_act(act, 0, U_FFN[0], 0, False)
            even_act(act)
            ffn_act(act, 1, U_FFN[1], 2, False)
            ffn_act(act, 2, U_FFN[2], 3, False)
            odd_act(act)
            ffn_act(act, 3, U_FFN[3], 5, True)
            norm_act(act, 6, 0)

        @block.vector
        def _(dve):
            dve.wait_ge(gain_in, 16)
            split_lo(dve, 0)
            for b in range(KD):
                lo_x(dve, 0, b)
            dve.wait_ge(const_in, 48)
            setup_dve(dve)
            ffn_dve(dve, 0, U_FFN[0], 0, False)
            even_dve(dve)
            ffn_dve(dve, 1, U_FFN[1], 2, False)
            ffn_dve(dve, 2, U_FFN[2], 3, False)
            odd_dve(dve)
            ffn_dve(dve, 3, U_FFN[3], 5, True)
            norm_dve(dve, 6)
            dve.wait_ge(rstd, 7)
            for b in range(KD):
                dve.wait_ge(sq_done, 8 * 7)
                nc.vector.scalar_tensor_tensor(x[:, b, :], x[:, b, :], gain[:, 6 * KD + b:6 * KD + b + 1],
                                               rB[:, :], ALU.mult, ALU.mult).then_inc(out_done, 1)


def unit_cols(w, width=256):
    k, n = w.shape
    return w.reshape(k // P, P, n // width, width).transpose(2, 1, 0, 3).reshape(-1, (k // P) * width)


def unit_rows(w):
    n, d = w.shape
    return w.reshape(n // 256, 2, P, d).transpose(0, 2, 1, 3).reshape(-1, 2 * d)


def unit_quarters(w):
    return w.reshape(2, 4, P, 2, 512).transpose(0, 3, 2, 1, 4).reshape(-1, UNIT)


def padded(a):
    return np.concatenate([a, np.zeros((a.shape[0], UNIT - a.shape[1]), a.dtype)], axis=1)


def ffn_units(wg, wu, wd):
    g, u = (unit_cols(w).reshape(PAIRS, 1, P, UNIT) for w in (wg, wu))
    return [np.concatenate([g, u], axis=1).reshape(-1, UNIT), unit_rows(wd)]


def channels(v):
    return v.reshape(-1, P).T


def rope_rows(dim, rows, first):
    inv = (1.0 / (np.float32(10000.0) ** (np.arange(0, dim, 2, dtype=np.float32) / np.float32(dim)))).astype(np.float32)
    ang = (inv[:, None] * np.arange(SEQ, dtype=np.float32)[None, :]).astype(np.float32)
    reps = 2 * (rows - first) // dim
    c, s = (np.concatenate([f] + [g(ang).astype(np.float32)] * reps) for f, g in
            ((np.ones((first, SEQ), np.float32), np.cos), (np.zeros((first, SEQ), np.float32), np.sin)))
    return np.concatenate([c, s])


def rope_perm(dim, rows, first):
    m = np.zeros((rows, rows), np.float32)
    for r in range(first, rows):
        if (r - first) % dim < dim // 2:
            m[r + dim // 2, r] = -1.0
        else:
            m[r - dim // 2, r] = 1.0
    return m


def window_masks():
    m = np.full((3, 16, 8, WIN), NEG, np.float32)
    for k, t in ((0, 0), (1, 1), (2, 3)):
        for c in range(16):
            lo = min(max(16 * t + c - 8, 0), GRID_C - 16) - WSTART[t]
            m[k, c, :, lo:lo + 16] = 0.0
    return m.transpose(1, 2, 0, 3).reshape(P, 3 * WIN)


def kernel(**inputs):
    import concourse.bacc as bacc
    from concourse.bass_utils import run_bass_kernel_spmd

    i = {k: np.asarray(v) for k, v in inputs.items()}
    ev, od = i["ev_w_in"][0], i["od_w_in"][0]
    parts = []
    parts += ffn_units(i["ffn1_wg"][0], i["ffn1_wu"][0], i["ffn1_wd"][0])
    parts += [unit_cols(ev), unit_quarters(i["ev_w_out"][0])]
    parts += ffn_units(i["ffn2_wg"][0], i["ffn2_wu"][0], i["ffn2_wd"][0])
    parts += ffn_units(i["ffn1_wg"][1], i["ffn1_wu"][1], i["ffn1_wd"][1])
    ckv_kr = np.concatenate([od[:, 1280:1408], od[:, 1344:1440], np.zeros((D, 32), od.dtype)], axis=1)
    gates = np.zeros((P, 2, 2, 4, P), od.dtype)
    for d in range(2):
        for k, w in enumerate((i["rg_wa"], i["rg_wx"])):
            for n in range(8):
                r = slice(64 * (n % 2), 64 * (n % 2) + 64)
                gates[r, d, k, n // 2, r] = w[0, d, n]
    uq = i["mla_wuq"][0].reshape(2, P, 768).transpose(1, 0, 2).reshape(P, 1536)
    parts += [unit_cols(od[:, 0:512]), unit_cols(od[:, 1024:1280]), unit_cols(ckv_kr), gates.reshape(P, UNIT),
              unit_cols(od[:, 512:1024]), padded(uq), padded(i["mla_wukv"][0]), unit_rows(i["od_w_out"][0])]
    parts += ffn_units(i["ffn2_wg"][1], i["ffn2_wu"][1], i["ffn2_wd"][1])
    units = np.concatenate(parts)
    assert units.shape == (N_UNITS * P, UNIT)

    norms = [i["ffn1_norm"][0], i["mix_norm"][0], i["ffn2_norm"][0], i["ffn1_norm"][1], i["mix_norm"][1],
             i["ffn2_norm"][1], i["final_norm"]]
    taps = np.concatenate([channels(i["conv_w"][0, j]) for j in range(4)], axis=1)
    colvec = np.concatenate([taps, channels(i["conv_b"][0]), channels(i["rg_ba"][0].reshape(-1)),
                             channels(i["rg_bx"][0].reshape(-1)), channels(i["rg_lam"][0].reshape(-1)),
                             channels(i["mla_gq"][0]), channels(i["mla_gkv"][0]), channels(i["diff_subln"][0])], axis=1)
    colvec = np.concatenate([colvec, np.zeros((P, 48 - colvec.shape[1]), colvec.dtype)], axis=1)
    small = np.zeros((P, 88), np.float32)
    small[:, 0] = EPS
    rpb = np.pad(i["na_rpb"][0][:, ::-1, ::-1], ((0, 0), (0, 0), (16, 17)))
    perm = np.zeros((P, P + 96), np.float32)
    perm[:, 0:P] = rope_perm(64, P, 0)
    perm[0:96, P:] = rope_perm(32, 96, 64)
    arrays = {
        "xT": i["x"][0].T, "units": units, "gains": np.concatenate([channels(g) for g in norms], axis=1),
        "consts": small, "colvec": colvec, "lamvec": i["diff_lam"][0].reshape(-1), "rpb": rpb.reshape(-1),
        "ident": np.eye(P, dtype=np.float32), "perm": perm, "rope_a": rope_rows(64, P, 0),
        "rope_d": rope_rows(32, 96, 64), "masks": window_masks(),
    }
    arrays = {k: np.ascontiguousarray(v) for k, v in arrays.items()}
    nc = bacc.Bacc("TRN2", target_bir_lowering=False, num_devices=1)
    args = [nc.dram_tensor("in_" + k, v.shape, mybir.dt.from_np(v.dtype), kind="ExternalInput").ap() for k, v in arrays.items()]
    args.append(nc.dram_tensor("outT", (D, SEQ), F32, kind="ExternalOutput").ap())
    build_trunk(nc, *args)
    r = run_bass_kernel_spmd(nc, [{"in_" + k: v for k, v in arrays.items()}], core_ids=[0])
    return np.ascontiguousarray(r.results[0]["outT"].T)[None]
```
